# Optimizing a Trainium2 kernel written in Bass

```python
import math
import jax, jax.numpy as jnp
from jax import lax
import numpy as np

D_MODEL = 1024
BATCH = 1
SEQ = 512
DEPTH = 2

CHUNK = 64
HEAD_DIM = 64
N_HEADS = (D_MODEL // 2) // HEAD_DIM
N_KV_HEADS = N_HEADS // 4
Q_PER_KV = N_HEADS // N_KV_HEADS
ATTN_WIDTH = N_HEADS * HEAD_DIM
KV_WIDTH = N_KV_HEADS * HEAD_DIM
WINDOW = 128
WINDOW_CHUNKS = WINDOW // CHUNK
POOL_WINDOWS = (2, 4, 8, 16)
POOL_GROUPS = len(POOL_WINDOWS)
POOL_WIDTH = D_MODEL // 2
POOL_GROUP_DIM = POOL_WIDTH // POOL_GROUPS
D_FF = ((8 * D_MODEL // 3 + 255) // 256) * 256
IN_WIDTH = ATTN_WIDTH + 2 * KV_WIDTH + POOL_WIDTH + 2 * D_MODEL
ROPE_THETA = 10000.0
EPS = 1e-6
N_ADA = 9

kernel_name = "hybrid_swa_sink_pool_macaron_adaln"

def _rmsnorm(x, g):
    xf = x.astype(jnp.float32)
    y = xf * lax.rsqrt(jnp.mean(xf * xf, axis=-1, keepdims=True) + EPS)
    return (y * g.astype(jnp.float32)).astype(x.dtype)

def _modulate(xn, shift, scale):
    return xn * (1 + scale[:, None, :]) + shift[:, None, :]

def _swiglu(u, w_up, w_down):
    a, b = jnp.split(u @ w_up, 2, axis=-1)
    return (jax.nn.silu(a) * b) @ w_down

def _rope_tables(positions, dtype):
    inv_freq = ROPE_THETA ** (-jnp.arange(0, HEAD_DIM, 2, dtype=jnp.float32) / HEAD_DIM)
    ang = positions.astype(jnp.float32)[..., None] * inv_freq
    return (jnp.cos(ang)[:, :, None, :].astype(dtype),
            jnp.sin(ang)[:, :, None, :].astype(dtype))

def _rope(x, cos, sin):
    half = HEAD_DIM // 2
    x1, x2 = x[..., :half], x[..., half:]
    return jnp.concatenate([x1 * cos - x2 * sin, x2 * cos + x1 * sin], axis=-1)

def _window_attention(q, k, v, sinks):
    B, S = q.shape[0], q.shape[1]
    n_chunks = S // CHUNK
    qc = q.reshape(B, n_chunks, CHUNK, N_KV_HEADS, Q_PER_KV, HEAD_DIM)

    def band(t):
        tc = t.reshape(B, n_chunks, CHUNK, N_KV_HEADS, HEAD_DIM)
        pad = jnp.zeros((B, WINDOW_CHUNKS - 1, CHUNK, N_KV_HEADS, HEAD_DIM), t.dtype)
        tp = jnp.concatenate([pad, tc], axis=1)
        return jnp.concatenate([tp[:, j:j + n_chunks] for j in range(WINDOW_CHUNKS)], axis=2)

    kb, vb = band(k), band(v)
    s = jnp.einsum("bcqhgd,bckhd->bhgcqk", qc, kb).astype(jnp.float32) * (HEAD_DIM ** -0.5)
    key_chunk = jnp.arange(n_chunks)[:, None] + (jnp.arange(WINDOW) // CHUNK)[None, :] - (WINDOW_CHUNKS - 1)
    valid = (key_chunk >= 0)[None, None, None, :, None, :]
    s = jnp.where(valid, s, -jnp.inf)
    sink = sinks.astype(jnp.float32).reshape(1, N_KV_HEADS, Q_PER_KV, 1, 1, 1)
    m = jnp.maximum(jnp.max(s, axis=-1, keepdims=True), sink)
    e = jnp.exp(s - m)
    probs = e / (jnp.sum(e, axis=-1, keepdims=True) + jnp.exp(sink - m))
    o = jnp.einsum("bhgcqk,bckhd->bcqhgd", probs.astype(v.dtype), vb)
    return o.reshape(B, S, ATTN_WIDTH)

def _multiscale_pool(p, w_group, scale):
    B, S = p.shape[0], p.shape[1]
    pf = p.astype(jnp.float32).reshape(B, S, POOL_GROUPS, POOL_GROUP_DIM)
    csum = jnp.cumsum(pf, axis=1)
    pos = jnp.arange(S)
    means = []
    for gi, w in enumerate(POOL_WINDOWS):
        cg = csum[:, :, gi]
        lagged = jnp.pad(cg, ((0, 0), (w, 0), (0, 0)))[:, :S]
        count = jnp.minimum(pos + 1, w).astype(jnp.float32)
        means.append((cg - lagged) / count[None, :, None])
    mixed = (jnp.stack(means, axis=2) - pf).astype(p.dtype)
    y = jnp.einsum("bsgi,gio->bsgo", mixed, w_group).reshape(B, S, POOL_WIDTH)
    return y * scale

def _token_mixing(u, w_in, q_norm_g, k_norm_g, sinks, w_pool_grp, pool_scale,
                  w_attn_o, w_pool_o, w_out, cos, sin):
    B, S = u.shape[0], u.shape[1]
    z = u @ w_in
    i1 = ATTN_WIDTH
    i2 = i1 + KV_WIDTH
    i3 = i2 + KV_WIDTH
    i4 = i3 + POOL_WIDTH
    i5 = i4 + D_MODEL
    q, k, v, p, g_a, g_p = jnp.split(z, [i1, i2, i3, i4, i5], axis=-1)
    q = _rope(_rmsnorm(q.reshape(B, S, N_HEADS, HEAD_DIM), q_norm_g), cos, sin)
    k = _rope(_rmsnorm(k.reshape(B, S, N_KV_HEADS, HEAD_DIM), k_norm_g), cos, sin)
    v = v.reshape(B, S, N_KV_HEADS, HEAD_DIM)
    y_attn = _window_attention(q, k, v, sinks) @ w_attn_o
    y_pool = _multiscale_pool(p, w_pool_grp, pool_scale) @ w_pool_o
    merged = jax.nn.sigmoid(g_a) * y_attn + jax.nn.sigmoid(g_p) * y_pool
    return merged @ w_out

def setup_inputs(seed: int = 0) -> dict:
    key = jax.random.key(seed)
    ks = jax.random.split(key, 20)
    f32 = jnp.float32

    def nrm(k, shape, scale):
        return jax.random.normal(k, shape, f32) * scale

    x = nrm(ks[0], (BATCH, SEQ, D_MODEL), 1.0)
    c = nrm(ks[1], (BATCH, D_MODEL), 1.0)
    start = jax.random.randint(ks[2], (BATCH, 1), 0, 64, dtype=jnp.int32) * CHUNK
    positions = start + jnp.arange(SEQ, dtype=jnp.int32)[None, :]
    return {
        "x": x,
        "c": c,
        "positions": positions,
        "w_ada": nrm(ks[3], (DEPTH, D_MODEL, N_ADA * D_MODEL), 0.5 * D_MODEL ** -0.5),
        "b_ada": nrm(ks[4], (DEPTH, N_ADA * D_MODEL), 0.02),
        "norm_g": 1.0 + nrm(ks[5], (DEPTH, 3, D_MODEL), 0.05),
        "w_ff1_up": nrm(ks[6], (DEPTH, D_MODEL, 2 * D_FF), D_MODEL ** -0.5),
        "w_ff1_down": nrm(ks[7], (DEPTH, D_FF, D_MODEL), D_FF ** -0.5),
        "w_in": nrm(ks[8], (DEPTH, D_MODEL, IN_WIDTH), D_MODEL ** -0.5),
        "q_norm_g": 1.0 + nrm(ks[9], (DEPTH, HEAD_DIM), 0.05),
        "k_norm_g": 1.0 + nrm(ks[10], (DEPTH, HEAD_DIM), 0.05),
        "sinks": nrm(ks[11], (DEPTH, N_HEADS), 0.5),
        "w_pool_grp": nrm(ks[12], (DEPTH, POOL_GROUPS, POOL_GROUP_DIM, POOL_GROUP_DIM), POOL_GROUP_DIM ** -0.5),
        "pool_scale": 1.0 + nrm(ks[13], (DEPTH, POOL_WIDTH), 0.1),
        "w_attn_o": nrm(ks[14], (DEPTH, ATTN_WIDTH, D_MODEL), ATTN_WIDTH ** -0.5),
        "w_pool_o": nrm(ks[15], (DEPTH, POOL_WIDTH, D_MODEL), POOL_WIDTH ** -0.5),
        "w_out": nrm(ks[16], (DEPTH, D_MODEL, D_MODEL), D_MODEL ** -0.5),
        "w_ff2_up": nrm(ks[17], (DEPTH, D_MODEL, 2 * D_FF), D_MODEL ** -0.5),
        "w_ff2_down": nrm(ks[18], (DEPTH, D_FF, D_MODEL), D_FF ** -0.5),
    }

def reference(x, c, positions, w_ada, b_ada, norm_g, w_ff1_up, w_ff1_down, w_in,
              q_norm_g, k_norm_g, sinks, w_pool_grp, pool_scale, w_attn_o, w_pool_o,
              w_out, w_ff2_up, w_ff2_down):
    B = x.shape[0]
    cos, sin = _rope_tables(positions, x.dtype)
    c_act = jax.nn.silu(c)
    for l in range(DEPTH):
        ada = (c_act @ w_ada[l] + b_ada[l]).reshape(B, N_ADA, D_MODEL)
        u = _modulate(_rmsnorm(x, norm_g[l, 0]), ada[:, 0], ada[:, 1])
        x = x + 0.5 * ada[:, 2][:, None, :] * _swiglu(u, w_ff1_up[l], w_ff1_down[l])
        u = _modulate(_rmsnorm(x, norm_g[l, 1]), ada[:, 3], ada[:, 4])
        mix = _token_mixing(u, w_in[l], q_norm_g[l], k_norm_g[l], sinks[l], w_pool_grp[l],
                            pool_scale[l], w_attn_o[l], w_pool_o[l], w_out[l], cos, sin)
        x = x + ada[:, 5][:, None, :] * mix
        u = _modulate(_rmsnorm(x, norm_g[l, 2]), ada[:, 6], ada[:, 7])
        x = x + 0.5 * ada[:, 8][:, None, :] * _swiglu(u, w_ff2_up[l], w_ff2_down[l])
    return x


_drawn_inputs = setup_inputs


def setup_inputs(seed=0):
    import zlib

    import numpy as np

    out = dict(_drawn_inputs(seed))
    spreads = {}
    factors = {'norm_g': 2.914, 'q_norm_g': 8.0, 'k_norm_g': 8.0, 'sinks': 8.0}
    for name, (base, spread) in spreads.items():
        noise = np.random.default_rng([zlib.crc32(name.encode()), seed]).standard_normal(out[name].shape)
        drawn = base * np.exp(spread * noise) if base else spread * noise
        out[name] = __import__('jax').numpy.asarray(drawn.astype(out[name].dtype))
    for name, factor in factors.items():
        out[name] = (out[name] * factor).astype(out[name].dtype)
    return out
```

```python
from contextlib import ExitStack

import numpy as np

import concourse.bass as bass
from concourse import mybir

F32 = mybir.dt.float32
F32R = mybir.dt.float32r
I32 = mybir.dt.int32
ALU = mybir.AluOpType
ACT = mybir.ActivationFunctionType
AX_X = mybir.AxisListType.X

P = 128
D = 1024
S = 512
DEPTH = 2
CHUNK = 64
N_CHUNKS = S // CHUNK
HEAD = 64
N_HEADS = 8
N_KV = 2
QPK = N_HEADS // N_KV
POOL_WINDOWS = (2, 4, 8, 16)
PAD = max(POOL_WINDOWS)
D_FF = 2816
N_ADA = 9
EPS = 1e-6
ROPE_THETA = 10000.0

KT = D // P
JT = S // P
HALF_FT = D_FF // P // 2
ATTN_W = N_HEADS * HEAD
KV_W = N_KV * HEAD
POOL_W = D // 2
Q_OFF, K_OFF = 0, ATTN_W
P_OFF = ATTN_W + 2 * KV_W
GA_OFF = P_OFF + POOL_W
GP_OFF = GA_OFF + D

STAGE_SLOTS, BANKS = 3, 5
STAGE_W = HALF_FT * 2 * P
HI_W = HALF_FT * P
AHEAD = 3

FF_TILES = 2 * HALF_FT + KT
FF_LOADS = FF_TILES // 2
T_Q, T_K, T_V, T_P = 0, 4, 5, 6
T_GA = T_P + len(POOL_WINDOWS)
T_GP = T_GA + KT
T_Y = T_GP + KT
T_OUT = T_Y + 2 * KT
MIX_TILES = T_OUT + KT
MIX_LOADS = ([(0, 2), (2, 2), (4, 2)] + [(T_P + g, 1) for g in range(4)]
             + [(t, 2) for t in range(T_GA, MIX_TILES, 2)])
TILES = 4 * FF_TILES + MIX_TILES
LOADS = 4 * FF_LOADS + len(MIX_LOADS)
assert FF_TILES % BANKS == 0 and MIX_TILES % BANKS == 0
assert FF_LOADS % STAGE_SLOTS == 0 and len(MIX_LOADS) % STAGE_SLOTS == 0

LOADED = 64

C_ADA, C_NORM, C_POOL, C_QG, C_KG = 0, N_ADA * KT, N_ADA * KT + 3 * KT, N_ADA * KT + 3 * KT + 4, N_ADA * KT + 3 * KT + 5
C_C = C_KG + 1
N_ROWS = C_C + KT

ADA_W = 512
FF_ADA = 3 * 2 * (KT // 2)
MIX_ADA = 3 * 2 * KT
ADA_PIECES = 4 * FF_ADA + MIX_ADA
FF_GROUPS, MIX_GROUPS = 6, 6
ADA_GROUPS = 4 * FF_GROUPS + MIX_GROUPS

NEWTON = 12
VEC_STEPS = 2 + 3 * 5
QK = (T_K, 0, 1, 2, 3)
ATT0 = T_P + 5
SOFT = 6 * N_CHUNKS


def soft_a(a):
    return 6 * a + 3


K_ID, K_SWAP, K_HEADS, K_FREQ, K_SIGN, K_CNT = 0, P, 2 * P, 2 * P + 2, 2 * P + 3, 2 * P + 4
K_W = K_CNT + len(POOL_WINDOWS) * PAD

TWO_PI_1 = 6.28125
TWO_PI_2 = float(np.float32(np.round((2 * np.pi - TWO_PI_1) * 2.0**20) / 2.0**20))
TWO_PI_3 = float(np.float32(2 * np.pi - TWO_PI_1 - TWO_PI_2))
ROUND = 12582912.0
SIN_MAX = 3.1415925


def shape_constants():
    k = np.zeros((P, K_W), np.float32)
    row = np.arange(P)
    k[row, K_ID + row] = 1.0
    k[row, K_SWAP + (row // HEAD) * HEAD + (row % HEAD + HEAD // 2) % HEAD] = 1.0
    k[row, K_HEADS + row // HEAD] = 1.0
    inv = (ROPE_THETA ** (-np.arange(0, HEAD, 2, dtype=np.float64) / HEAD)).astype(np.float32)
    k[:, K_FREQ] = inv[row % (HEAD // 2)]
    k[:, K_SIGN] = np.where(row % HEAD < HEAD // 2, -1.0, 1.0)
    for g, w in enumerate(POOL_WINDOWS):
        k[:, K_CNT + g * PAD:K_CNT + (g + 1) * PAD] = 1.0 / np.minimum(np.arange(PAD) + 1, w)
    return k


def trunk(nc, x, c, positions, w_ada, b_ada, norm_g, w_ff1_up, w_ff1_down, w_in, q_norm_g, k_norm_g,
          sinks, w_pool_grp, pool_scale, w_attn_o, w_pool_o, w_out, w_ff2_up, w_ff2_down, consts, out):
    ctx = ExitStack()
    with ctx:
        place = [nc.sbuf_base + (-nc.sbuf_base) % 64]

        def region(nbytes):
            at = place[0]
            place[0] += nbytes + (-nbytes) % 32
            return at

        def at(name, shape, dt, offset):
            return nc.alloc_sbuf_tensor_at(name, shape, dt, offset=offset)

        KB2 = S * 4
        r_stage = region(STAGE_SLOTS * STAGE_W * 4)
        r_hi = region(BANKS * HI_W * 4)
        r_x = region(KT * KB2)
        r_u = region(2 * KT * KB2)
        r_h = region(2 * HALF_FT * KB2)
        r_g = region(KT * KB2)
        r_e = region(4 * KB2)
        r_a = region(3 * (PAD + S) * 4)
        r_misc = region(7 * KB2)

        stage = [at(f"stage{s}", [P, STAGE_W], F32, r_stage + s * STAGE_W * 4) for s in range(STAGE_SLOTS)]
        w_lo = [at(f"w_lo{s}", [P, STAGE_W], F32R, r_stage + s * STAGE_W * 4) for s in range(STAGE_SLOTS)]
        w_hi = [at(f"w_hi{s}", [P, HI_W], F32R, r_hi + s * HI_W * 4) for s in range(BANKS)]
        x_t = at("x_t", [P, KT, S], F32, r_x)
        u_hi = at("u_hi", [P, KT, S], F32R, r_u)
        u_lo = at("u_lo", [P, KT, S], F32R, r_u + KT * KB2)
        x_rows = at("x_rows", [P, JT, D], F32, r_u)
        out_rows = at("out_rows", [P, JT, D], F32, r_u + KT * KB2)
        h_hi = at("h_hi", [P, HALF_FT, S], F32R, r_h)
        h_lo = at("h_lo", [P, HALF_FT, S], F32R, r_h + HALF_FT * KB2)
        LO = HALF_FT - KT
        q_rot = at("q_rot", [P, N_CHUNKS, QPK, CHUNK], F32, r_h + KT * KB2)
        k_rot = at("k_rot", [P, N_KV, S], F32, r_h + (KT + QPK) * KB2)
        ADA_FIRST = 2 * HALF_FT // 2
        ada_first = [at(f"ada_first{s}", [P, D], F32, r_h + s * D * 4) for s in range(ADA_FIRST)]
        gate_a = at("gate_a", [P, KT, S], F32, r_g)
        qk_raw = at("qk_raw", [P, 5, S], F32, r_g + 3 * KB2)
        silu = at("silu", [P, 2, S], F32, r_g)
        prod = at("prod", [P, 2, S], F32, r_g + 2 * KB2)
        xn = at("xn", [P, 2, S], F32, r_g + 4 * KB2)
        u_f = at("u_f", [P, 2, S], F32, r_g + 6 * KB2)
        rope_a = at("rope_a", [P, S], F32, r_e)
        rope_b = at("rope_b", [P, S], F32, r_e + KB2)
        rstd_b = at("rstd_b", [P, S], F32, r_e + 2 * KB2)
        pool_y = at("pool_y", [P, S], F32, r_e + 3 * KB2)
        v_t = at("v_t", [P, S], F32, r_e + 3 * KB2)
        merge = at("merge", [P, 2, S], F32, r_e)
        gate_p = ([at(f"gate_p{i}", [P, S], F32, r_stage + i * STAGE_W * 4 + KT * 2 * P * 4) for i in range(3)]
                  + [at(f"gate_p{3 + i}", [P, S], F32, r_e + (2 + i) * KB2) for i in range(2)]
                  + [at(f"gate_p{5 + i}", [P, S], F32, r_a + i * KB2) for i in range(3)])
        pool_in = at("pool_in", [P, PAD + S], F32, r_a)
        pool_s = [at(f"pool_s{i}", [P, PAD + S], F32, r_a + (1 + i) * (PAD + S) * 4) for i in range(2)]
        probs = [at(f"probs{i}", [P, 4, P], F32, r_a + i * KB2) for i in range(2)]
        probs_t = at("probs_t", [P, 4 * P], F32, r_a + 2 * KB2)
        r = r_misc
        cos_t = at("cos_t", [P, S], F32, r)
        sin_t = at("sin_t", [P, S], F32, r + KB2)
        squares = at("squares", [P, S], F32, r + 2 * KB2)
        sq_sum = at("sq_sum", [P, S], F32, r + 3 * KB2)
        v_win = at("v_win", [P, N_CHUNKS, P], F32, r + 4 * KB2)
        pool_w = at("pool_w", [P, 4, P], F32, r + 6 * KB2)
        ada_stage = [at(f"ada_stage{i}", [P, ADA_W], F32, region(ADA_W * 4)) for i in range(2)]
        ada_acc = at("ada_acc", [P, ADA_W], F32, region(ADA_W * 4))
        ada_acc0 = at("ada_acc0", [P, D], F32, r + 4 * KB2)
        consts_s = at("consts_s", [P, K_W], F32, region(K_W * 4))
        ones = at("ones", [P, 1], F32, region(32))
        rows = at("rows", [P, DEPTH, P], F32, r_g)
        pos_i = at("pos_i", [P, S], I32, r_g + KB2)
        angle = at("angle", [P, S], F32, r_g + 2 * KB2)
        turns = at("turns", [P, S], F32, r_g + 3 * KB2)
        vec = at("vec", [P, DEPTH, N_ROWS], F32, region(DEPTH * N_ROWS * 4))
        lay = at("lay", [P, N_ROWS], F32, region(N_ROWS * 4))
        sink_all = at("sink_all", [P, DEPTH, 4], F32, region(DEPTH * 16))
        neg_sink = at("neg_sink", [P, 4], F32, region(32))
        c_half = at("c_half", [P, KT // 2], F32, region(32))
        c_act = at("c_act", [P, KT], F32, region(KT * 4))
        ada_sum = at("ada_sum", [P, N_ADA, KT], F32, region(N_ADA * KT * 4))
        ada_vec = at("ada_vec", [P, 3, KT], F32, region(3 * KT * 4))
        shift = at("shift", [P, 3, KT], F32, region(3 * KT * 4))
        scale = at("scale", [P, 3, KT], F32, region(3 * KT * 4))
        gate = at("gate", [P, 3, KT], F32, region(3 * KT * 4))
        nw_v = at("nw_v", [P, 40], F32, region(160))
        nw_y = at("nw_y", [P, 40], F32, region(160))
        nw_t = at("nw_t", [P, 40], F32, region(160))
        neg_max = at("neg_max", [P, 2, 4], F32, region(32))
        row_max = at("row_max", [P, 4], F32, region(32))
        sink_d = at("sink_d", [P, 2, 4], F32, region(32))
        e_sum = at("e_sum", [P, 2, 4], F32, region(32))
        e_sink = at("e_sink", [P, 2, 4], F32, region(32))
        den = at("den", [P, 4], F32, region(32))
        inv_den = at("inv_den", [P, 4], F32, region(32))
        edge = at("edge", [P, PAD], F32, region(PAD * 4))
        assert place[0] <= nc.sbuf_usable_end, (place[0], nc.sbuf_usable_end)

        ident = consts_s[:, K_ID:K_ID + P]
        swap = consts_s[:, K_SWAP:K_SWAP + P]
        heads = consts_s[:, K_HEADS:K_HEADS + 2]

        bank = [ctx.enter_context(nc.psum_tensor(f"bank{i}", [P, S], F32)) for i in range(BANKS)]
        ps5, ps6, ps7 = [ctx.enter_context(nc.psum_tensor(f"ps{i}", [P, S], F32)) for i in (5, 6, 7)]

        def sem(name):
            return ctx.enter_context(nc.semaphore(name))

        consts_in = sem("consts_in")
        x_in = sem("x_in")
        ada_first_in = [sem(f"ada_first_in{s}") for s in range(ADA_FIRST)]
        loaded = [sem(f"loaded{s}") for s in range(STAGE_SLOTS)]
        ada_in = [sem(f"ada_in{i}") for i in range(2)]
        pool_w_in = sem("pool_w_in")
        hi_ready = sem("hi_ready")
        lo_ready = sem("lo_ready")
        tile_done = sem("tile_done")
        product_ready = sem("product_ready")
        silu_ready = sem("silu_ready")
        h_hi_ready = sem("h_hi_ready")
        h_lo_ready = sem("h_lo_ready")
        x_updated = sem("x_updated")
        squared = sem("squared")
        squares_added = sem("squares_added")
        norm_summed = sem("norm_summed")
        newton = sem("newton")
        rstd_spread = sem("rstd_spread")
        xn_ready = sem("xn_ready")
        u_hi_ready = sem("u_hi_ready")
        u_f_ready = sem("u_f_ready")
        u_lo_ready = sem("u_lo_ready")
        vec_step = sem("vec_step")
        ada_used = sem("ada_used")
        ada_reduced = sem("ada_reduced")
        ada_added = sem("ada_added")
        mix_read = sem("mix_read")
        gate_read = sem("gate_read")
        qk_squared = sem("qk_squared")
        qk_summed = sem("qk_summed")
        v_turned = sem("v_turned")
        v_kept = sem("v_kept")
        rstd_copied = sem("rstd_copied")
        qk_spread = sem("qk_spread")
        qk_normed = sem("qk_normed")
        qk_swapped = sem("qk_swapped")
        rope_step = sem("rope_step")
        pads_zeroed = sem("pads_zeroed")
        pool_step = sem("pool_step")
        pool_mixed = sem("pool_mixed")
        pool_grouped = sem("pool_grouped")
        pool_y_step = sem("pool_y_step")
        scored = sem("scored")
        soft_step = sem("soft_step")
        exp_ready = sem("exp_ready")
        probs_zeroed = sem("probs_zeroed")
        probs_turned = sem("probs_turned")
        probs_kept = sem("probs_kept")
        attended = sem("attended")
        attn_step = sem("attn_step")
        merge_step = sem("merge_step")
        turned = sem("turned")
        turned_kept = sem("turned_kept")
        turned_kept_act = sem("turned_kept_act")
        first_reduced = sem("first_reduced")
        setup_step = sem("setup_step")
        ada_first_used = sem("ada_first_used")
        ada_first_done = sem("ada_first_done")
        c_half_ready = sem("c_half_ready")
        act_step = sem("act_step")
        rows_turned = sem("rows_turned")
        stored = sem("stored")

        def tiles_before(l, i, half=0):
            return l * TILES + (0, 2 * FF_TILES, 2 * FF_TILES + MIX_TILES)[i] + half * FF_TILES

        def loads_before(l, i, half=0):
            per = (0, 2 * FF_LOADS, 2 * FF_LOADS + len(MIX_LOADS))
            return l * (LOADS // STAGE_SLOTS) + per[i] // STAGE_SLOTS + half * (FF_LOADS // STAGE_SLOTS)

        def x_before(l, i, half=0):
            return KT + l * 5 * KT + (0, 2 * KT, 3 * KT)[i] + half * KT

        def adds_before(l, i, half=0):
            return (KT - 2) + l * 5 * (KT - 2) + (0, 2, 3)[i] * (KT - 2) + half * (KT - 2)

        def products_before(l, i, half):
            return l * 4 * HALF_FT + (0, 0, 2)[i] * HALF_FT + half * HALF_FT

        def pieces_before(l, i, half=0):
            return l * ADA_PIECES + (0, 2 * FF_ADA, 2 * FF_ADA + MIX_ADA)[i] + half * FF_ADA

        def groups_before(l, i, half=0):
            return l * ADA_GROUPS + (0, 2 * FF_GROUPS, 2 * FF_GROUPS + MIX_GROUPS)[i] + half * FF_GROUPS

        def newton_before(l, i):
            return (l * 4 + i) * NEWTON

        DONE = BANKS + 1

        def ff_load_of(n):
            return n // 2, n % 2

        MIX_LOAD_OF = {t + j: (i, j) for i, (t, k) in enumerate(MIX_LOADS) for j in range(k)}

        def depth(kind, n):
            if kind == "ff":
                return KT if n < 2 * HALF_FT or n >= FF_TILES else HALF_FT
            return QPK if T_Y <= n < T_OUT else KT

        def slot_of(kind, n):
            if kind == "ff" or n >= MIX_TILES:
                if kind == "mix":
                    i, j = ff_load_of(n - MIX_TILES)
                    i += len(MIX_LOADS)
                else:
                    i, j = ff_load_of(n)
            else:
                i, j = MIX_LOAD_OF[n]
            return i % STAGE_SLOTS, i // STAGE_SLOTS + 1, j

        def stage_tile(t, kind, n):
            s, _, j = slot_of(kind, n)
            k = depth(kind, n)
            return t[s][:, 0:k * 2 * P].rearrange("p (k c) -> p k c", c=2 * P)[:, :, j * P:(j + 1) * P]

        def hi_tile(n, k):
            return w_hi[n % BANKS][:, 0:k * P].rearrange("p (k c) -> p k c", c=P)

        block = ctx.enter_context(nc.Block())

        @block.sync
        def _(sp):
            def ff_half(l, i, half, up, down):
                up_v = up.rearrange("l (k p) n -> l p k n", p=P)
                down_v = down.rearrange("l (f p) n -> l p f n", p=P)
                sent = 0
                for n in range(FF_LOADS):
                    s = n % STAGE_SLOTS
                    dst = stage[s][:, :].rearrange("p (k c) -> p k c", c=2 * P)
                    sp.wait_ge(tile_done, tiles_before(l, i, half) + 2 * n - 5 + DONE)
                    if n < HALF_FT:
                        for j in range(2):
                            sp.dma_start(dst[:, 0:KT, j * P:(j + 1) * P],
                                         up_v[l, :, :, bass.ds((half * HALF_FT + n) * P + j * D_FF, P)]
                                         ).then_inc(loaded[s], LOADED // 2)
                    else:
                        m = 2 * (n - HALF_FT)
                        sp.dma_start(dst[:, :, :], down_v[l, :, bass.ds(half * HALF_FT, HALF_FT), m * P:(m + 2) * P]
                                     ).then_inc(loaded[s], LOADED)
                    while sent < FF_ADA and sent <= 2 * n - 2:
                        ada_piece(l, i, half, sent)
                        sent += 1
                assert sent == FF_ADA

            def ada_piece(l, i, half, a):
                per = KT if i == 1 else KT // 2
                g, k = divmod(a, per)
                row = k if i == 1 else half * (KT // 2) + k
                src = w_ada.rearrange("l (k p) n -> l k p n", p=P)
                free = pieces_before(l, i, half) + a + 1
                if i < 2:
                    sp.wait_ge(ada_used, free)
                    sp.dma_start(ada_stage[a % 2][:, :],
                                 src[l, row, :, (3 * (i + 1) * 2 + g) * ADA_W:(3 * (i + 1) * 2 + g + 1) * ADA_W]
                                 ).then_inc(ada_in[a % 2], 16)
                else:
                    with sp.If(l < DEPTH - 1):
                        sp.wait_ge(ada_used, free)
                        sp.dma_start(ada_stage[a % 2][:, :], src[DEPTH - 1, row, :, g * ADA_W:(g + 1) * ADA_W]
                                     ).then_inc(ada_in[a % 2], 16)
                    with sp.Else():
                        sp.wait_ge(ada_used, free)
                        sp.sem_inc(ada_in[a % 2], 16)

            def mix(l):
                in_v = w_in.rearrange("l (k p) n -> l p k n", p=P)
                ao_v = w_attn_o.rearrange("l (g t p) n -> l g p t n", g=N_KV, p=HEAD)
                po_v = w_pool_o.rearrange("l (g p) n -> l p g n", p=P)
                out_v = w_out.rearrange("l (k p) n -> l p k n", p=P)
                sent = 0
                for n, (t, k) in enumerate(MIX_LOADS):
                    s = n % STAGE_SLOTS
                    dst = stage[s][:, 0:KT * 2 * P].rearrange("p (k c) -> p k c", c=2 * P)
                    if n < STAGE_SLOTS:
                        last = 2 * n - 5
                    else:
                        last = sum(MIX_LOADS[n - STAGE_SLOTS]) - 1
                    sp.wait_ge(tile_done, tiles_before(l, 1) + last + DONE)
                    if t < T_K:
                        for j in range(2):
                            for g in range(N_KV):
                                col = Q_OFF + (g * QPK + t + j) * HEAD
                                sp.dma_start(dst[:, :, j * P + g * HEAD:j * P + (g + 1) * HEAD],
                                             in_v[l, :, :, col:col + HEAD]).then_inc(loaded[s], LOADED // 4)
                    elif t < T_Y:
                        col = {T_K: K_OFF}.get(t, P_OFF + (t - T_P) * P)
                        sp.dma_start(dst[:, :, 0:k * P], in_v[l, :, :, col:col + k * P]).then_inc(loaded[s], LOADED)
                    elif t < T_OUT:
                        m = (t - T_Y) // 2
                        for g in range(N_KV):
                            sp.dma_start(dst[g * HEAD:(g + 1) * HEAD, 0:QPK, 0:P],
                                         ao_v[l, g, :, :, m * P:(m + 1) * P]).then_inc(loaded[s], LOADED // 4)
                        sp.dma_start(dst[:, 0:4, P:2 * P], po_v[l, :, :, m * P:(m + 1) * P]
                                     ).then_inc(loaded[s], LOADED // 2)
                    else:
                        sp.dma_start(dst[:, :, :], out_v[l, :, :, (t - T_OUT) * P:(t - T_OUT + 2) * P]
                                     ).then_inc(loaded[s], LOADED)
                    if n == 0:
                        sp.dma_start(pool_w[:, :, :], w_pool_grp.rearrange("l g i o -> l i g o")[l]
                                     ).then_inc(pool_w_in, 16)
                    while sent < MIX_ADA and sent <= t - 2:
                        ada_piece(l, 1, 0, sent)
                        sent += 1
                while sent < MIX_ADA:
                    ada_piece(l, 1, 0, sent)
                    sent += 1

            sp.dma_start(consts_s[:, :], consts).then_inc(consts_in, 16)
            for l in range(DEPTH):
                for first, src in ((C_ADA, b_ada[l].rearrange("(r c) -> r c", c=P)),
                                   (C_NORM, norm_g[l].rearrange("n (r c) -> (n r) c", c=P)),
                                   (C_POOL, pool_scale[l].rearrange("(r c) -> r c", c=P)),
                                   (C_C, c.rearrange("b (r c) -> (b r) c", c=P))):
                    sp.dma_start(rows[first:first + src.shape[0], l, :], src).then_inc(consts_in, 16)
                for row, src in ((C_QG, q_norm_g), (C_KG, k_norm_g)):
                    for g in range(2):
                        sp.dma_start(rows[row:row + 1, l, g * HEAD:(g + 1) * HEAD], src[l:l + 1, :]
                                     ).then_inc(consts_in, 16)
                with nc.allow_non_contiguous_dma(reason="eight sinks"):
                    for t in range(2):
                        sp.dma_start(sink_all[t * CHUNK:(t + 1) * CHUNK, l, :],
                                     sinks[l].rearrange("(b t) -> t b", t=2)[t].partition_broadcast(CHUNK)
                                     ).then_inc(consts_in, 16)
            sp.dma_start(pos_i[:, :], positions[0].partition_broadcast(P)).then_inc(consts_in, 16)
            sp.dma_start(x_rows[:, :, :], x.rearrange("b (j p) d -> p (b j) d", p=P)).then_inc(x_in, 16)
            for a in range(3 * KT):
                v, k = divmod(a, KT)
                if a >= ADA_FIRST:
                    sp.wait_ge(ada_first_used, a - ADA_FIRST + 1)
                sp.dma_start(ada_first[a % ADA_FIRST][:, :], w_ada[0, k * P:(k + 1) * P, v * D:(v + 1) * D]
                             ).then_inc(ada_first_in[a % ADA_FIRST], 16)

            with sp.Fori(0, DEPTH) as l:
                with sp.Fori(0, 2) as half:
                    ff_half(l, 0, half, w_ff1_up, w_ff1_down)
                mix(l)
                with sp.Fori(0, 2) as half:
                    ff_half(l, 2, half, w_ff2_up, w_ff2_down)
            for j in range(JT):
                sp.wait_ge(turned_kept, j + 1)
                sp.wait_ge(turned_kept_act, j + 1)
                sp.dma_start(out[0, j * P:(j + 1) * P, :], out_rows[:, j, :]).then_inc(stored, 16)
            sp.wait_ge(stored, 16 * JT)

        N_CONSTS = 16 * (1 + DEPTH * 10 + 1)

        @block.gpsimd
        def _(pool):
            def low_part(kind, base, n):
                pool.wait_ge(hi_ready, base + n + 1)
                t = stage_tile(stage, kind, n)
                nc.gpsimd.tensor_tensor(stage_tile(w_lo, kind, n), t, hi_tile(n, depth(kind, n)),
                                        ALU.subtract).then_inc(lo_ready, 1)

            def window_sums(l, g):
                pool.wait_ge(mix_read, l * 26 + T_P + g + 1)
                src = pool_in
                for i in range(g + 1):
                    step = 1 << i
                    done = l * 10 + g * (g + 1) // 2 + i
                    if i:
                        pool.wait_ge(pool_step, done)
                    nc.gpsimd.tensor_tensor(pool_s[i % 2][:, PAD:], src[:, PAD:], src[:, PAD - step:PAD + S - step],
                                            ALU.add).then_inc(pool_step, 1)
                    src = pool_s[i % 2]

            nc.gpsimd.memset(ones[:, :], 1.0).then_inc(pads_zeroed, 1)
            with pool.Fori(0, DEPTH) as l:
                with pool.Fori(0, 2) as half:
                    for n in range(FF_TILES):
                        low_part("ff", tiles_before(l, 0, half), n)
                for n in range(MIX_TILES):
                    low_part("mix", tiles_before(l, 1), n)
                    if n == T_K:
                        for t in (pool_in, *pool_s):
                            nc.gpsimd.memset(t[:, 0:PAD], 0.0).then_inc(pads_zeroed, 1)
                        pool.wait_ge(pads_zeroed, l * 3 + 4)
                    if T_P + 2 <= n < T_P + 6:
                        window_sums(l, n - T_P - 2)
                with pool.Fori(0, 2) as half:
                    for n in range(FF_TILES):
                        low_part("ff", tiles_before(l, 2, half), n)
            for s in range((AHEAD + 1) // 2):
                pool.wait_ge(tile_done, DEPTH * TILES + 2 * s - 5 + DONE)
                nc.gpsimd.memset(stage[s][:, 0:KT * 2 * P], 0.0).then_inc(loaded[s], LOADED)

        @block.scalar
        def _(act):
            def round_weights(kind, tiles, loads, n):
                s, count, _ = slot_of(kind, n)
                act.wait_ge(loaded[s], LOADED * (loads + count))
                act.wait_ge(tile_done, tiles + n - BANKS + DONE)
                nc.scalar.activation(hi_tile(n, depth(kind, n)), stage_tile(stage, kind, n), ACT.Copy
                                     ).then_inc(hi_ready, 1)

            def square(x_count, m, adds):
                act.wait_ge(x_updated, x_count + m + 1)
                if m == 0:
                    dst = sq_sum
                else:
                    dst = squares
                    if m > 1:
                        act.wait_ge(squares_added, adds + m - 1)
                nc.scalar.activation(dst[:, :], x_t[:, m, :], ACT.Square).then_inc(squared, 1)

            def modulate(l, i):
                for k in range(KT):
                    act.wait_ge(xn_ready, (l * 3 + i) * KT + k + 1)
                    if k >= 2:
                        act.wait_ge(u_lo_ready, (l * 3 + i) * KT + k - 1)
                    for dst, ready in ((u_hi[:, k, :], u_hi_ready), (u_f[:, k % 2, :], u_f_ready)):
                        nc.scalar.activation(dst, xn[:, k % 2, :], ACT.Identity, scale=scale[:, i, k:k + 1],
                                             bias=shift[:, i, k:k + 1]).then_inc(ready, 1)

            def ff_half(l, i, half):
                tiles, loads = tiles_before(l, i, half), loads_before(l, i, half)
                for n in range(FF_TILES):
                    round_weights("ff", tiles, loads, n + AHEAD)
                    if n < 2 * HALF_FT and n % 2 == 0:
                        j = n // 2
                        act.wait_ge(tile_done, tiles + n + DONE)
                        if j >= 2:
                            act.wait_ge(product_ready, products_before(l, i, half) + j - 1)
                        nc.scalar.activation(silu[:, j % 2, :], bank[n % BANKS][:, :], ACT.Silu
                                             ).then_inc(silu_ready, 1)
                    if n >= 2 * HALF_FT:
                        square(x_before(l, i, half), n - 2 * HALF_FT, adds_before(l, i, half))

            def attend(l, a):
                if 1 <= a <= N_CHUNKS:
                    act.wait_ge(probs_turned, l * N_CHUNKS + a)
                    nc.scalar.activation(probs_t[:, :], ps6[:, :], ACT.Copy).then_inc(probs_kept, 1)
                if a < N_CHUNKS:
                    keys = slice(0, CHUNK) if a == 0 else slice(0, 2 * CHUNK)
                    act.wait_ge(soft_step, l * SOFT + soft_a(a))
                    for b in range(4):
                        nc.scalar.activation(probs[a % 2][:, b, keys], ps5[:, b * P:(b + 1) * P][:, keys], ACT.Exp,
                                             scale=HEAD ** -0.5, bias=neg_max[:, a % 2, b:b + 1],
                                             accum_out=e_sum[:, a % 2, b:b + 1]).then_inc(exp_ready, 1)
                    nc.scalar.activation(e_sink[:, a % 2, :], sink_d[:, a % 2, :], ACT.Exp).then_inc(exp_ready, 1)

            def mix(l):
                tiles, loads = tiles_before(l, 1), loads_before(l, 1)
                for n in range(MIX_TILES):
                    round_weights("mix", tiles, loads, n + AHEAD)
                    if n == T_P:
                        for h in range(2):
                            act.wait_ge(v_turned, l * 2 + h + 1)
                            nc.scalar.activation(v_win[:, 4 * h:4 * h + 4, :].rearrange("p c d -> p (c d)"),
                                                 (ps6, ps7)[h][:, :], ACT.Copy).then_inc(v_kept, 1)
                    if n < 5:
                        act.wait_ge(mix_read, l * 26 + n + 1)
                        if n:
                            act.wait_ge(qk_summed, l * 5 + n)
                        nc.scalar.activation(squares[:, :], qk_raw[:, n, :], ACT.Square).then_inc(qk_squared, 1)
                    if T_GA <= n < T_Y:
                        g = n - T_GA
                        act.wait_ge(tile_done, tiles + n + DONE)
                        dst = gate_a[:, g, :] if g < KT else gate_p[g - KT][:, :]
                        if 3 <= g < KT:
                            act.wait_ge(rope_step, l * 15 + 15)
                        nc.scalar.activation(dst, bank[n % BANKS][:, :], ACT.Tanh, scale=0.5
                                             ).then_inc(gate_read, 1)
                    if ATT0 <= n < ATT0 + N_CHUNKS + 2:
                        attend(l, n - ATT0)
                    if n >= T_OUT:
                        square(x_before(l, 1), n - T_OUT, adds_before(l, 1))

            act.wait_ge(setup_step, DEPTH)
            nc.scalar.activation(c_act[:, :], vec[:, 0, C_C:C_C + KT], ACT.Silu).then_inc(act_step, 1)
            act.wait_ge(setup_step, DEPTH + 8)
            nc.scalar.activation(sin_t[:, :], angle[:, :], ACT.Sin).then_inc(act_step, 1)
            nc.scalar.activation(cos_t[:, :], angle[:, :], ACT.Sin, scale=0.5).then_inc(act_step, 1)
            for m in range(KT):
                square(0, m, 0)
            for n in range(AHEAD):
                s, count, _ = slot_of("ff", n)
                act.wait_ge(loaded[s], LOADED * count)
                nc.scalar.activation(hi_tile(n, KT), stage_tile(stage, "ff", n), ACT.Copy).then_inc(hi_ready, 1)
            with act.Fori(0, DEPTH) as l:
                modulate(l, 0)
                with act.Fori(0, 2) as half:
                    ff_half(l, 0, half)
                modulate(l, 1)
                mix(l)
                modulate(l, 2)
                with act.Fori(0, 2) as half:
                    ff_half(l, 2, half)
            for j in range(JT):
                act.wait_ge(turned, KT + 2 * j + 2)
                nc.scalar.activation(out_rows[:, j, D // 2:], (ps5, ps7)[j % 2][:, :], ACT.Copy
                                     ).then_inc(turned_kept_act, 1)

        @block.vector
        def _(dve):
            def rsqrt(count, src, width, over):
                v, y, t = nw_v[:, 0:width], nw_y[:, 0:width], nw_t[:, 0:width]
                nc.vector.tensor_scalar(v, src, 1.0 / over, EPS, ALU.mult, ALU.add).then_inc(newton, 1)
                dve.wait_ge(newton, count + 1)
                nc.vector.tensor_scalar(y.bitcast(I32), v.bitcast(I32), 1, None, ALU.logical_shift_right
                                        ).then_inc(newton, 1)
                dve.wait_ge(newton, count + 2)
                nc.vector.tensor_scalar(y.bitcast(I32), y.bitcast(I32), -1.0, float(0x5F3759DF), ALU.mult, ALU.add
                                        ).then_inc(newton, 1)
                for i in range(3):
                    dve.wait_ge(newton, count + 3 + 3 * i)
                    nc.vector.tensor_tensor(t, y, y, ALU.mult).then_inc(newton, 1)
                    dve.wait_ge(newton, count + 4 + 3 * i)
                    nc.vector.scalar_tensor_tensor(t, t, -0.5, v, ALU.mult, ALU.mult).then_inc(newton, 1)
                    dve.wait_ge(newton, count + 5 + 3 * i)
                    nc.vector.scalar_tensor_tensor(y, t, 1.5, y, ALU.add, ALU.mult).then_inc(newton, 1)

            def vectors(l, i):
                count = l * VEC_STEPS + 2 + i * 5
                dve.wait_ge(ada_added, groups_before(l, i) + 1)
                s = ada_sum[:, 3 * i:3 * i + 3, :]
                b = lay[:, C_ADA + 3 * i * KT:C_ADA + 3 * (i + 1) * KT].rearrange("p (v k) -> p v k", k=KT)
                dve.wait_ge(vec_step, count)
                nc.vector.tensor_tensor(ada_vec[:, :, :], s, b, ALU.add).then_inc(vec_step, 1)
                dve.wait_ge(vec_step, count + 1)
                nc.vector.tensor_copy(shift[:, i, :], ada_vec[:, 0, :]).then_inc(vec_step, 1)
                nc.vector.scalar_tensor_tensor(scale[:, i, :], ada_vec[:, 1, :], 1.0,
                                               lay[:, C_NORM + i * KT:C_NORM + (i + 1) * KT], ALU.add, ALU.mult
                                               ).then_inc(vec_step, 1)
                nc.vector.tensor_scalar(gate[:, i, :], ada_vec[:, 2, :], 0.5, None, ALU.mult).then_inc(vec_step, 1)
                nc.vector.memset(s, 0.0).then_inc(vec_step, 1)

            def normalise(l, i):
                dve.wait_ge(norm_summed, l * 3 + i + 1)
                count = newton_before(l, (0, 1, 3)[i])
                rsqrt(count, ps5[:, 0:JT], JT, D)
                dve.wait_ge(rstd_spread, l * 3 + i + 1)
                base = (l * 3 + i) * KT

                def low(k):
                    dve.wait_ge(u_f_ready, base + k + 1)
                    nc.vector.tensor_tensor(u_lo[:, k, :], u_f[:, k % 2, :], u_hi[:, k, :], ALU.subtract
                                            ).then_inc(u_lo_ready, 1)
                for k in range(KT):
                    if k >= 2:
                        low(k - 2)
                    nc.vector.tensor_tensor(xn[:, k % 2, :], x_t[:, k, :], ps6[:, :], ALU.mult).then_inc(xn_ready, 1)
                low(KT - 2)
                low(KT - 1)

            def update_x(l, i, half, m, n, tiles):
                dve.wait_ge(tile_done, tiles + n + DONE)
                nc.vector.scalar_tensor_tensor(x_t[:, m, :], bank[n % BANKS][:, :], gate[:, i, m:m + 1], x_t[:, m, :],
                                               ALU.mult, ALU.add).then_inc(x_updated, 1)
                if m >= 2:
                    add_squares(x_before(l, i, half), m - 1, adds_before(l, i, half))

            def add_squares(x_count, m, adds):
                dve.wait_ge(squared, x_count + m + 1)
                if m >= 2:
                    dve.wait_ge(squares_added, adds + m - 1)
                nc.vector.tensor_tensor(sq_sum[:, :], sq_sum[:, :], squares[:, :], ALU.add).then_inc(squares_added, 1)

            def ada_piece(l, i, half, a):
                count, per = pieces_before(l, i, half), KT if i == 1 else KT // 2
                k = a % per
                row = k if i == 1 else half * (KT // 2) + k
                dve.wait_ge(ada_in[a % 2], 16 * (l * (ADA_PIECES // 2) + (0, FF_ADA, FF_ADA + MIX_ADA // 2)[i]
                                                 + half * (FF_ADA // 2) + a // 2 + 1))
                c_k = c_act[:, k:k + 1] if i == 1 else c_half[:, k:k + 1]
                if k == 0:
                    dve.wait_ge(ada_reduced, groups_before(l, i, half) + a // per + 1)
                    nc.vector.tensor_scalar(ada_acc[:, :], ada_stage[a % 2][:, :], c_k, None, ALU.mult
                                            ).then_inc(ada_used, 1)
                else:
                    dve.wait_ge(ada_used, count + a + 2)
                    nc.vector.scalar_tensor_tensor(ada_acc[:, :], ada_stage[a % 2][:, :], c_k, ada_acc[:, :],
                                                   ALU.mult, ALU.add).then_inc(ada_used, 1)

            def ada_group(l, i, half, g):
                count = groups_before(l, i, half) + g
                dve.wait_ge(ada_reduced, count + 2)
                v = 3 * (i + 1) % N_ADA + g // 2
                s = ada_sum[:, v, (g % 2) * 4:(g % 2) * 4 + 4]
                nc.vector.tensor_tensor(s, s, ps7[:, 0:4], ALU.add).then_inc(ada_added, 1)

            def ff_half(l, i, half):
                tiles = tiles_before(l, i, half)
                count = products_before(l, i, half)
                half_count = l * 4 + (0, 0, 2)[i] + half
                nc.vector.tensor_copy(c_half[:, :], c_act[:, bass.ds(half * (KT // 2), KT // 2)]
                                      ).then_inc(c_half_ready, 1)
                dve.wait_ge(c_half_ready, half_count + 1)
                for n in range(FF_TILES):
                    if n < 2 * HALF_FT and n % 2 == 1:
                        j = n // 2
                        dve.wait_ge(silu_ready, count + j + 1)
                        dve.wait_ge(tile_done, tiles + n + DONE)
                        if j:
                            dve.wait_ge(h_lo_ready, count + j)
                        nc.vector.tensor_tensor(prod[:, j % 2, :], silu[:, j % 2, :], bank[n % BANKS][:, :], ALU.mult
                                                ).then_inc(product_ready, 1)
                        dve.wait_ge(product_ready, count + j + 1)
                        nc.vector.tensor_copy(h_hi[:, j, :], prod[:, j % 2, :]).then_inc(h_hi_ready, 1)
                        dve.wait_ge(h_hi_ready, count + j + 1)
                        nc.vector.tensor_tensor(h_lo[:, j, :], prod[:, j % 2, :], h_hi[:, j, :], ALU.subtract
                                                ).then_inc(h_lo_ready, 1)
                    if n >= 2 * HALF_FT:
                        update_x(l, i, half, n - 2 * HALF_FT, n, tiles)
                    if n and n % 4 == 0 and n // 4 <= FF_GROUPS:
                        ada_group(l, i, half, n // 4 - 1)
                    if n < FF_ADA:
                        ada_piece(l, i, half, n)

            def read_tile(tiles, n, dst):
                dve.wait_ge(tile_done, tiles + n + DONE)
                nc.vector.tensor_copy(dst, bank[n % BANKS][:, :]).then_inc(mix_read, 1)

            def widen_rstd(l, i):
                if i:
                    dve.wait_ge(qk_spread, l * 5 + i)
                nc.vector.tensor_copy(rstd_b[:, :].rearrange("p (j c) -> p j c", c=HEAD),
                                      nw_y[:, 8 * QK[i]:8 * QK[i] + 8].unsqueeze(2).to_broadcast([P, 8, HEAD])
                                      ).then_inc(rstd_copied, 1)

            def norm_qk(l, i):
                dve.wait_ge(qk_spread, l * 5 + i + 1)
                g = C_KG if QK[i] == T_K else C_QG
                raw = qk_raw[:, QK[i], :]
                nc.vector.scalar_tensor_tensor(raw, ps6[:, :], lay[:, g:g + 1], raw, ALU.mult, ALU.mult
                                               ).then_inc(qk_normed, 1)

            def rope(l, i):
                count = l * 15 + 3 * i
                if i:
                    dve.wait_ge(rope_step, count)
                dve.wait_ge(qk_swapped, l * 5 + i + 1)
                nc.vector.tensor_tensor(rope_a[:, :], qk_raw[:, QK[i], :], cos_t[:, :], ALU.mult
                                        ).then_inc(rope_step, 1)
                nc.vector.tensor_tensor(rope_b[:, :], ps7[:, :], sin_t[:, :], ALU.mult).then_inc(rope_step, 1)
                dve.wait_ge(rope_step, count + 2)
                if QK[i] == T_K:
                    for g in range(N_KV):
                        r = slice(g * HEAD, (g + 1) * HEAD)
                        ins = nc.vector.tensor_tensor(k_rot[r, g, :], rope_a[r, :], rope_b[r, :], ALU.add)
                    ins.then_inc(rope_step, 1)
                else:
                    v = "p (c q) -> p c q"
                    nc.vector.tensor_tensor(q_rot[:, :, QK[i], :], rope_a[:, :].rearrange(v, q=CHUNK),
                                            rope_b[:, :].rearrange(v, q=CHUNK), ALU.add).then_inc(rope_step, 1)

            def pool_mix(l, g):
                dve.wait_ge(pool_step, l * 10 + (g + 1) * (g + 2) // 2)
                s, count = pool_s[g % 2], (l * 4 + g) * 3
                nc.vector.tensor_tensor(edge[:, :], s[:, PAD:2 * PAD], consts_s[:, K_CNT + g * PAD:K_CNT + (g + 1) * PAD],
                                        ALU.mult).then_inc(pool_mixed, 1)
                nc.vector.scalar_tensor_tensor(pool_in[:, 2 * PAD:], s[:, 2 * PAD:], 1.0 / POOL_WINDOWS[g],
                                               pool_in[:, 2 * PAD:], ALU.mult, ALU.subtract).then_inc(pool_mixed, 1)
                dve.wait_ge(pool_mixed, count + 2)
                nc.vector.tensor_tensor(pool_in[:, PAD:2 * PAD], edge[:, :], pool_in[:, PAD:2 * PAD], ALU.subtract
                                        ).then_inc(pool_mixed, 1)

            def pool_out(l, g):
                dve.wait_ge(pool_grouped, l * 4 + g + 1)
                count = (l * 4 + g) * 3
                nc.vector.tensor_scalar(pool_y[:, :], ps5[:, :], lay[:, C_POOL + g:C_POOL + g + 1], None, ALU.mult
                                        ).then_inc(pool_y_step, 1)
                dve.wait_ge(pool_y_step, count + 1)
                nc.vector.tensor_copy(h_hi[:, 4 + g, :], pool_y[:, :]).then_inc(pool_y_step, 1)
                dve.wait_ge(pool_y_step, count + 2)
                nc.vector.tensor_tensor(h_lo[:, LO + 4 + g, :], pool_y[:, :], h_hi[:, 4 + g, :], ALU.subtract
                                        ).then_inc(pool_y_step, 1)

            def attend(l, a):
                base = l * SOFT
                if a < N_CHUNKS:
                    keys = slice(0, CHUNK) if a == 0 else slice(0, 2 * CHUNK)
                    at_a = base + soft_a(a)
                    dve.wait_ge(scored, l * N_CHUNKS + a + 1)
                    nc.vector.tensor_reduce(row_max[:, :], ps5[:, :].rearrange("p (b k) -> p b k", k=P)[:, :, keys],
                                            AX_X, ALU.max).then_inc(soft_step, 1)
                    dve.wait_ge(soft_step, at_a - 2)
                    nc.vector.scalar_tensor_tensor(neg_max[:, a % 2, :], row_max[:, :], -(HEAD ** -0.5), neg_sink[:, :],
                                                   ALU.mult, ALU.min).then_inc(soft_step, 1)
                    dve.wait_ge(soft_step, at_a - 1)
                    nc.vector.tensor_tensor(sink_d[:, a % 2, :], neg_max[:, a % 2, :], neg_sink[:, :], ALU.subtract
                                            ).then_inc(soft_step, 1)
                if a >= 2:
                    ch = a - 2
                    dve.wait_ge(attended, l * N_CHUNKS + ch + 1)
                    count = (l * N_CHUNKS + ch) * 4
                    for g in range(N_KV):
                        r = slice(g * HEAD, (g + 1) * HEAD)
                        o = ps7[r, g * 256:(g + 1) * 256].rearrange("p (t q) -> p t q", q=CHUNK)
                        dst = h_hi[r, 0:QPK, ch * CHUNK:(ch + 1) * CHUNK]
                        nc.vector.tensor_copy(dst, o).then_inc(attn_step, 1)
                        dve.wait_ge(attn_step, count + 2 * g + 1)
                        nc.vector.tensor_tensor(h_lo[r, LO:LO + QPK, ch * CHUNK:(ch + 1) * CHUNK], o, dst, ALU.subtract
                                                ).then_inc(attn_step, 1)
                if a < N_CHUNKS:
                    dve.wait_ge(exp_ready, (l * N_CHUNKS + a + 1) * 5)
                    nc.vector.tensor_tensor(den[:, :], e_sum[:, a % 2, :], e_sink[:, a % 2, :], ALU.add
                                            ).then_inc(soft_step, 1)
                    dve.wait_ge(soft_step, at_a + 1)
                    nc.vector.reciprocal(inv_den[:, :], den[:, :]).then_inc(soft_step, 1)
                    dve.wait_ge(soft_step, at_a + 2)
                    p = probs[a % 2][:, :, keys]
                    w = CHUNK if a == 0 else 2 * CHUNK
                    nc.vector.tensor_tensor(p, p, inv_den[:, :].unsqueeze(2).to_broadcast([P, 4, w]), ALU.mult
                                            ).then_inc(soft_step, 1)

            def merged(l, n, tiles):
                m, which = divmod(n - T_Y, 2)
                count = (l * KT + m) * 4
                dve.wait_ge(tile_done, tiles + n + DONE)
                if which == 0:
                    if m == 0:
                        dve.wait_ge(gate_read, (l + 1) * 2 * KT)
                    else:
                        dve.wait_ge(merge_step, count)
                    nc.vector.scalar_tensor_tensor(merge[:, 0, :], gate_a[:, m, :], 1.0, bank[n % BANKS][:, :],
                                                   ALU.add, ALU.mult).then_inc(mix_read, 1)
                    return
                nc.vector.scalar_tensor_tensor(merge[:, 1, :], gate_p[m][:, :], 1.0, bank[n % BANKS][:, :],
                                               ALU.add, ALU.mult).then_inc(mix_read, 1)
                dve.wait_ge(mix_read, l * 26 + 10 + (n - T_Y) + 1)
                nc.vector.tensor_tensor(merge[:, 0, :], merge[:, 0, :], merge[:, 1, :], ALU.add).then_inc(merge_step, 2)
                dve.wait_ge(merge_step, count + 2)
                nc.vector.tensor_copy(u_hi[:, m, :], merge[:, 0, :]).then_inc(merge_step, 1)
                dve.wait_ge(merge_step, count + 3)
                nc.vector.tensor_tensor(u_lo[:, m, :], merge[:, 0, :], u_hi[:, m, :], ALU.subtract
                                        ).then_inc(merge_step, 1)

            def mix(l):
                tiles = tiles_before(l, 1)
                for n in range(MIX_TILES):
                    if T_P + 1 <= n <= T_P + 4:
                        rope(l, n - T_P - 1)
                        norm_qk(l, n - T_P)
                        if n - T_P + 1 < 5:
                            widen_rstd(l, n - T_P + 1)
                    if T_P + 1 <= n <= T_P + 3:
                        pool_mix(l, n - T_P - 1)
                    if n == T_P + 5:
                        pool_out(l, 3)
                    if n == 16:
                        ada_group(l, 1, 0, 1)
                    if n < 5:
                        read_tile(tiles, n, qk_raw[:, n, :])
                    if n == T_V:
                        read_tile(tiles, n, v_t[:, :])
                        nc.vector.memset(k_rot[HEAD:, 0, :], 0.0)
                        nc.vector.memset(k_rot[0:HEAD, 1, :], 0.0)
                        dve.wait_ge(qk_summed, (l + 1) * 5)
                        rsqrt(newton_before(l, 2), ps5[:, 0:40], 40, HEAD)
                        dve.wait_ge(newton, newton_before(l, 2) + NEWTON)
                        widen_rstd(l, 0)
                    if T_P <= n < T_P + 4:
                        if n == T_P:
                            dve.wait_ge(pads_zeroed, l * 3 + 4)
                        else:
                            dve.wait_ge(pool_grouped, l * 4 + n - T_P)
                        read_tile(tiles, n, pool_in[:, PAD:])
                    if n == T_P:
                        norm_qk(l, 0)
                        widen_rstd(l, 1)
                    if T_P + 1 <= n <= T_P + 3:
                        pool_out(l, n - T_P - 1)
                    if n == T_P + 4:
                        rope(l, 4)
                        pool_mix(l, 3)
                    if n == ATT0:
                        dve.wait_ge(pool_grouped, (l + 1) * 4)
                        nc.vector.memset(probs[0][:, :, CHUNK:], 0.0).then_inc(probs_zeroed, 1)
                    if ATT0 <= n < ATT0 + N_CHUNKS + 2:
                        attend(l, n - ATT0)
                    if T_Y <= n < T_OUT:
                        merged(l, n, tiles)
                    if n >= T_OUT:
                        update_x(l, 1, 0, n - T_OUT, n, tiles)
                    if n and n % 8 == 0 and n != 16:
                        ada_group(l, 1, 0, n // 8 - 1)
                    if n < MIX_ADA:
                        ada_piece(l, 1, 0, n)

            dve.sem_inc(ada_used, 2)
            dve.wait_ge(consts_in, N_CONSTS)
            for l in range(DEPTH):
                dve.wait_ge(rows_turned, l + 1)
                nc.vector.tensor_copy(vec[:, l, :], (ps5, ps6)[l][:, 0:N_ROWS]).then_inc(setup_step, 1)
            dve.wait_ge(setup_step, DEPTH)
            nc.vector.tensor_copy(angle[:, :], pos_i[:, :]).then_inc(setup_step, 1)
            dve.wait_ge(setup_step, DEPTH + 1)
            nc.vector.tensor_scalar(angle[:, :], angle[:, :], consts_s[:, K_FREQ:K_FREQ + 1], None, ALU.mult
                                    ).then_inc(setup_step, 1)
            dve.wait_ge(setup_step, DEPTH + 2)
            nc.vector.tensor_scalar(turns[:, :], angle[:, :], float(1.0 / (2 * np.pi)), ROUND, ALU.mult, ALU.add
                                    ).then_inc(setup_step, 1)
            dve.wait_ge(setup_step, DEPTH + 3)
            nc.vector.tensor_scalar(turns[:, :], turns[:, :], ROUND, None, ALU.subtract).then_inc(setup_step, 1)
            for i, part in enumerate((TWO_PI_1, TWO_PI_2, TWO_PI_3)):
                dve.wait_ge(setup_step, DEPTH + 4 + i)
                nc.vector.scalar_tensor_tensor(angle[:, :], turns[:, :], -part, angle[:, :], ALU.mult, ALU.add
                                               ).then_inc(setup_step, 1)
            dve.wait_ge(setup_step, DEPTH + 7)
            nc.vector.tensor_scalar(angle[:, :], angle[:, :], SIN_MAX, -SIN_MAX, ALU.min, ALU.max).then_inc(setup_step, 1)
            dve.wait_ge(act_step, 3)
            nc.vector.tensor_scalar(sin_t[:, :], sin_t[:, :], consts_s[:, K_SIGN:K_SIGN + 1], None, ALU.mult
                                    ).then_inc(setup_step, 1)
            nc.vector.tensor_tensor(cos_t[:, :], cos_t[:, :], cos_t[:, :], ALU.mult).then_inc(setup_step, 1)
            dve.wait_ge(setup_step, DEPTH + 10)
            nc.vector.tensor_scalar(cos_t[:, :], cos_t[:, :], -2.0, 1.0, ALU.mult, ALU.add).then_inc(setup_step, 1)
            nc.vector.memset(ada_sum[:, :, :], 0.0).then_inc(setup_step, 1)
            dve.wait_ge(setup_step, DEPTH + 12)
            for m in range(KT):
                dve.wait_ge(turned, m + 1)
                nc.vector.tensor_copy(x_t[:, m, :], bank[m % 4][:, :]).then_inc(x_updated, 1)
                if m >= 2:
                    add_squares(0, m - 1, 0)
            for a in range(3 * KT):
                v, k = divmod(a, KT)
                dve.wait_ge(ada_first_in[a % ADA_FIRST], 16 * (a // ADA_FIRST + 1))
                if k == 0:
                    if v:
                        dve.wait_ge(first_reduced, v)
                    nc.vector.tensor_scalar(ada_acc0[:, :], ada_first[a % ADA_FIRST][:, :], c_act[:, k:k + 1], None,
                                            ALU.mult).then_inc(ada_first_used, 1)
                else:
                    dve.wait_ge(ada_first_used, a)
                    nc.vector.scalar_tensor_tensor(ada_acc0[:, :], ada_first[a % ADA_FIRST][:, :], c_act[:, k:k + 1],
                                                   ada_acc0[:, :], ALU.mult, ALU.add).then_inc(ada_first_used, 1)
                if k == KT - 1:
                    dve.wait_ge(first_reduced, v + 1)
                    nc.vector.tensor_copy(ada_sum[:, v, :], ps7[:, 0:KT]).then_inc(ada_first_done, 1)
            dve.wait_ge(ada_first_done, 3)
            dve.sem_inc(ada_added, 1)

            with dve.Fori(0, DEPTH) as l:
                nc.vector.tensor_copy(lay[:, :], vec[:, l, :]).then_inc(vec_step, 1)
                nc.vector.tensor_scalar(neg_sink[:, :], sink_all[:, l, :], -1.0, None, ALU.mult).then_inc(vec_step, 1)
                vectors(l, 0)
                normalise(l, 0)
                with dve.Fori(0, 2) as half:
                    ff_half(l, 0, half)
                vectors(l, 1)
                normalise(l, 1)
                mix(l)
                vectors(l, 2)
                normalise(l, 2)
                with dve.Fori(0, 2) as half:
                    ff_half(l, 2, half)
            for j in range(JT):
                dve.wait_ge(turned, KT + 2 * j + 1)
                nc.vector.tensor_copy(out_rows[:, j, 0:D // 2], (ps6, bank[0])[j % 2][:, :]).then_inc(turned_kept, 1)

        @block.tensor
        def _(pe):
            mm = nc.tensor.matmul

            def tile(kind, base, n, rhs_hi, rhs_lo, before=None, middle=None):
                k_n = depth(kind, n)
                hi, lo = hi_tile(n, k_n), stage_tile(w_lo, kind, n)
                pe.wait_ge(hi_ready, base + n + 1)
                pe.wait_ge(lo_ready, base + n + 1)
                for k in range(k_n):
                    if before:
                        before(k)
                    mm(bank[n % BANKS][:, :], hi[:, k, :], rhs_hi(k), start=(k == 0), stop=False)
                    mm(bank[n % BANKS][:, :], hi[:, k, :], rhs_lo(k), start=False, stop=False)
                    last = mm(bank[n % BANKS][:, :], lo[:, k, :], rhs_hi(k), start=False, stop=(k == k_n - 1))
                    if middle and k == k_n // 2 - 1:
                        middle()
                last.then_inc(tile_done, 1)

            def u_parts():
                return lambda k: u_hi[:, k, :], lambda k: u_lo[:, k, :]

            def norm_sum(l, i):
                pe.wait_ge(squares_added, adds_before(l, i))
                for j in range(JT):
                    mm(ps5[:, j:j + 1], sq_sum[:, j * P:(j + 1) * P], ones[:, :], start=(j == 0), stop=False,
                       skip_group_check=True)
                pe.wait_ge(squared, x_before(l, i))
                for j in range(JT):
                    last = mm(ps5[:, j:j + 1], squares[:, j * P:(j + 1) * P], ones[:, :], start=False, stop=True,
                              skip_group_check=True)
                last.then_inc(norm_summed, 1)

            def norm_spread(l, i):
                pe.wait_ge(newton, newton_before(l, (0, 1, 3)[i]) + NEWTON)
                for j in range(JT):
                    last = mm(ps6[:, j * P:(j + 1) * P], nw_y[:, j:j + 1].to_broadcast([P, P]), ident,
                              start=True, stop=True)
                last.then_inc(rstd_spread, 1)

            def norm(l, i):
                norm_sum(l, i)
                norm_spread(l, i)

            def first_u(l, i):
                return lambda k: pe.wait_ge(u_lo_ready, (l * 3 + i) * KT + k + 1)

            def ada_reduce(l, i, half, g):
                per = KT if i == 1 else KT // 2
                pe.wait_ge(ada_used, pieces_before(l, i, half) + (g + 1) * per + 2)
                pe.wait_ge(ada_added, groups_before(l, i, half) + g + 1)
                for m in range(4):
                    last = mm(ps7[:, m:m + 1], ada_acc[:, m * P:(m + 1) * P], ones[:, :], start=True, stop=True)
                last.then_inc(ada_reduced, 1)

            def ff_half(l, i, half):
                base = tiles_before(l, i, half)
                count = products_before(l, i, half)
                x_count = x_before(l, i, half)
                for n in range(FF_TILES):
                    if n < BANKS:
                        pe.wait_ge(x_updated, x_count + n - BANKS + 1)
                    elif n - BANKS < 2 * HALF_FT:
                        pe.wait_ge(product_ready, count + (n - BANKS) // 2 + 1)
                    else:
                        pe.wait_ge(x_updated, x_count + n - BANKS - 2 * HALF_FT + 1)
                    if n < 2 * HALF_FT:
                        tile("ff", base, n, *u_parts(), before=first_u(l, i) if n == 0 else None)
                    else:
                        tile("ff", base, n, lambda k: h_hi[:, k, :], lambda k: h_lo[:, k, :],
                             before=(lambda k: pe.wait_ge(h_lo_ready, count + k + 1)) if n == 2 * HALF_FT else None)
                    if n and n % 4 == 0 and n // 4 <= FF_GROUPS:
                        ada_reduce(l, i, half, n // 4 - 1)

            def qk_sum(l, t):
                pe.wait_ge(qk_squared, l * 5 + t + 1)
                for j in range(JT):
                    last = mm(ps5[:, 8 * t + 2 * j:8 * t + 2 * j + 2], squares[:, j * P:(j + 1) * P], heads,
                              start=(t == 0 and j == 0), stop=True, skip_group_check=True)
                last.then_inc(qk_summed, 1)

            def turn_v(l):
                pe.wait_ge(mix_read, l * 26 + T_V + 1)
                pe.wait_ge(ada_added, groups_before(l, 1) + 1)
                for h in range(2):
                    for c in range(4 * h, 4 * h + 4):
                        first = max(c - 1, 0) * CHUNK
                        last = nc.tensor.transpose((ps6, ps7)[h][:, (c % 4) * P:(c % 4 + 1) * P],
                                                   v_t[:, first:first + P], ident)
                    last.then_inc(v_turned, 1)

            def spread_qk(l, i):
                pe.wait_ge(rstd_copied, l * 5 + i + 1)
                if i == 0:
                    pe.wait_ge(v_kept, l * 2 + 2)
                else:
                    pe.wait_ge(qk_normed, l * 5 + i)
                for j in range(JT):
                    last = mm(ps6[:, j * P:(j + 1) * P], rstd_b[:, j * P:(j + 1) * P], ident, start=True, stop=True)
                last.then_inc(qk_spread, 1)

            def swap_qk(l, i):
                pe.wait_ge(qk_normed, l * 5 + i + 1)
                if i:
                    pe.wait_ge(rope_step, l * 15 + 3 * i - 1)
                if i == 2:
                    pe.wait_ge(ada_added, groups_before(l, 1) + 2)
                mm(ps7[:, :], swap, qk_raw[:, QK[i], :], start=True, stop=True).then_inc(qk_swapped, 1)

            def group_pool(l, g):
                pe.wait_ge(pool_mixed, (l * 4 + g + 1) * 3)
                if g == 0:
                    pe.wait_ge(pool_w_in, 16 * (l + 1))
                else:
                    pe.wait_ge(pool_y_step, (l * 4 + g) * 3)
                mm(ps5[:, :], pool_w[:, g, :], pool_in[:, PAD:], start=True, stop=True).then_inc(pool_grouped, 1)

            def attend(l, a):
                if a >= 2:
                    ch = a - 2
                    pe.wait_ge(probs_kept, l * N_CHUNKS + ch + 1)
                    if ch:
                        pe.wait_ge(attn_step, (l * N_CHUNKS + ch) * 4)
                    if a == 16 - ATT0:
                        pe.wait_ge(ada_added, groups_before(l, 1) + 3)
                    mm(ps7[:, :], v_win[:, ch, :], probs_t[:, :], start=True, stop=True).then_inc(attended, 1)
                if 1 <= a <= N_CHUNKS:
                    ch = a - 1
                    pe.wait_ge(soft_step, l * SOFT + soft_a(ch) + 3)
                    if ch == 0:
                        pe.wait_ge(probs_zeroed, l + 1)
                    for b in range(4):
                        last = nc.tensor.transpose(ps6[:, b * P:(b + 1) * P], probs[ch % 2][:, b, :], ident)
                    last.then_inc(probs_turned, 1)
                if a < N_CHUNKS:
                    if a == 0:
                        pe.wait_ge(rope_step, (l + 1) * 15)
                        pe.wait_ge(pool_y_step, (l + 1) * 12)
                    else:
                        pe.wait_ge(exp_ready, (l * N_CHUNKS + a) * 5)
                    first, keys = (0, CHUNK) if a == 0 else ((a - 1) * CHUNK, 2 * CHUNK)
                    for b in range(4):
                        g, pair = divmod(b, 2)
                        last = mm(ps5[:, b * P:b * P + keys], q_rot[:, a, 2 * pair:2 * pair + 2, :],
                                  k_rot[:, g, first:first + keys], start=True, stop=True)
                    last.then_inc(scored, 1)

            def mix(l):
                base, x_count = tiles_before(l, 1), x_before(l, 1)
                for n in range(MIX_TILES):
                    o = n - BANKS
                    if o < 0:
                        pe.wait_ge(x_updated, x_count + o + 1)
                    elif o < T_GA:
                        pe.wait_ge(mix_read, l * 26 + o + 1)
                    elif o < T_Y:
                        pe.wait_ge(gate_read, l * 2 * KT + o - T_GA + 1)
                    elif o < T_OUT:
                        pe.wait_ge(mix_read, l * 26 + 10 + o - T_Y + 1)
                    else:
                        pe.wait_ge(x_updated, x_count + o - T_OUT + 1)

                    def middle(n=n):
                        if n == T_P:
                            turn_v(l)
                        if T_P + 1 <= n <= T_P + 4:
                            swap_qk(l, n - T_P - 1)
                            spread_qk(l, n - T_P)
                        if n == T_P + 5:
                            group_pool(l, 3)
                        if n == 16:
                            pe.wait_ge(attn_step, (l * N_CHUNKS + 3) * 4)
                            ada_reduce(l, 1, 0, 1)

                    before = None
                    if n == 0:
                        before = first_u(l, 1)
                    if T_Y <= n < T_OUT:
                        part = 4 * ((n - T_Y) % 2)
                        if n == T_Y:
                            pe.wait_ge(attn_step, (l + 1) * N_CHUNKS * 4)
                        rhs = (lambda k, o=part: h_hi[:, o + k, :], lambda k, o=part: h_lo[:, LO + o + k, :])
                    else:
                        rhs = u_parts()
                    if n == T_OUT:
                        before = lambda k: pe.wait_ge(merge_step, (l * KT + k + 1) * 4)
                    tile("mix", base, n, *rhs, before=before, middle=middle)
                    if 1 <= n <= 5:
                        qk_sum(l, n - 1)
                    if n == T_P:
                        spread_qk(l, 0)
                    if T_P + 1 <= n <= T_P + 3:
                        group_pool(l, n - T_P - 1)
                    if n == T_P + 4:
                        swap_qk(l, 4)
                    if ATT0 <= n < ATT0 + N_CHUNKS + 2:
                        attend(l, n - ATT0)
                    if n == 8:
                        pe.wait_ge(rope_step, l * 15 + 5)
                    if n == 24:
                        pe.wait_ge(attn_step, (l + 1) * N_CHUNKS * 4)
                    if n and n % 8 == 0 and n != 16:
                        ada_reduce(l, 1, 0, n // 8 - 1)

            pe.sem_inc(tile_done, BANKS)
            pe.sem_inc(ada_reduced, 1)
            pe.wait_ge(consts_in, N_CONSTS)
            pe.wait_ge(pads_zeroed, 1)
            for l in range(DEPTH):
                nc.tensor.transpose((ps5, ps6)[l][:, 0:N_ROWS], rows[0:N_ROWS, l, :], ident[0:N_ROWS, 0:N_ROWS]
                                    ).then_inc(rows_turned, 1)
            pe.wait_ge(x_in, 16)
            for m in range(KT):
                if m >= 4:
                    pe.wait_ge(x_updated, m - 3)
                for j in range(JT):
                    last = nc.tensor.transpose(bank[m % 4][:, j * P:(j + 1) * P], x_rows[:, j, m * P:(m + 1) * P], ident)
                last.then_inc(turned, 1)
            for v in range(3):
                pe.wait_ge(ada_first_used, (v + 1) * KT)
                if v:
                    pe.wait_ge(ada_first_done, v)
                for m in range(KT):
                    last = mm(ps7[:, m:m + 1], ada_acc0[:, m * P:(m + 1) * P], ones[:, :], start=True, stop=True)
                last.then_inc(first_reduced, 1)

            with pe.Fori(0, DEPTH) as l:
                norm(l, 0)
                with pe.Fori(0, 2) as half:
                    ff_half(l, 0, half)
                norm(l, 1)
                mix(l)
                norm(l, 2)
                with pe.Fori(0, 2) as half:
                    ff_half(l, 2, half)
            pe.wait_ge(x_updated, KT + DEPTH * 5 * KT)
            pe.wait_ge(ada_added, DEPTH * ADA_GROUPS + 1)
            for j in range(JT):
                for h in range(2):
                    if j >= 2:
                        if h == 0:
                            pe.wait_ge(turned_kept, j - 1)
                        else:
                            pe.wait_ge(turned_kept_act, j - 1)
                    dst = ((ps6, bank[0]), (ps5, ps7))[h][j % 2]
                    for m in range(4):
                        last = nc.tensor.transpose(dst[:, m * P:(m + 1) * P],
                                                   x_t[:, 4 * h + m, j * P:(j + 1) * P], ident)
                    last.then_inc(turned, 1)


INPUTS = ["x", "c", "positions", "w_ada", "b_ada", "norm_g", "w_ff1_up", "w_ff1_down", "w_in", "q_norm_g",
          "k_norm_g", "sinks", "w_pool_grp", "pool_scale", "w_attn_o", "w_pool_o", "w_out", "w_ff2_up", "w_ff2_down"]


def kernel(**inputs):
    import concourse.bacc as bacc
    from concourse.bass_utils import run_bass_kernel_spmd

    nc = bacc.Bacc("TRN2", target_bir_lowering=False, num_devices=1)
    arrays = {f"in_{name}": np.ascontiguousarray(inputs[name]) for name in INPUTS}
    arrays["in_consts"] = shape_constants()
    args = [nc.dram_tensor(name, a.shape, mybir.dt.from_np(a.dtype), kind="ExternalInput").ap()
            for name, a in arrays.items()]
    out = nc.dram_tensor("out", (1, S, D), F32, kind="ExternalOutput").ap()
    trunk(nc, *args, out)
    result = run_bass_kernel_spmd(nc, [arrays], core_ids=[0])
    return result.results[0]["out"]
```

```python
from contextlib import ExitStack

import numpy as np

import concourse.bass as bass
from concourse import mybir

F32 = mybir.dt.float32
F32R = mybir.dt.float32r
I32 = mybir.dt.int32
ALU = mybir.AluOpType
ACT = mybir.ActivationFunctionType
AX_X = mybir.AxisListType.X

P = 128
D = 1024
S = 512
DEPTH = 2
CHUNK = 64
N_CHUNKS = S // CHUNK
HEAD = 64
N_HEADS = 8
N_KV = 2
QPK = N_HEADS // N_KV
POOL_WINDOWS = (2, 4, 8, 16)
PAD = max(POOL_WINDOWS)
D_FF = 2816
N_ADA = 9
EPS = 1e-6
ROPE_THETA = 10000.0

KT = D // P
JT = S // P
HALF_FT = D_FF // P // 2
ATTN_W = N_HEADS * HEAD
KV_W = N_KV * HEAD
POOL_W = D // 2
Q_OFF, K_OFF = 0, ATTN_W
P_OFF = ATTN_W + 2 * KV_W
GA_OFF = P_OFF + POOL_W

STAGE_SLOTS, BANKS = 3, 5
STAGE_W = HALF_FT * 2 * P
HI_W = HALF_FT * P
AHEAD = 3

FF_TILES = 2 * HALF_FT + KT
FF_LOADS = FF_TILES // 2
T_K, T_V, T_P = 4, 5, 6
T_GA = T_P + len(POOL_WINDOWS)
T_GP = T_GA + KT
T_Y = T_GP + KT
T_OUT = T_Y + 2 * KT
MIX_TILES = T_OUT + KT
MIX_LOADS = ([(t, 2) for t in range(0, T_GA, 2)]
             + [(T_GA + 5 * j + t, k) for j in range(3) for t, k in ((0, 1), (1, 2), (3, 2))] + [(T_Y - 1, 1)]
             + [(t, 2) for t in range(T_Y, MIX_TILES, 2)])
assert all(a + k == b for (a, k), (b, _) in zip(MIX_LOADS, MIX_LOADS[1:]))
TILES = 4 * FF_TILES + MIX_TILES
LOADS = 4 * FF_LOADS + len(MIX_LOADS)
assert FF_TILES % BANKS == 0 and MIX_TILES % BANKS == 0
assert FF_LOADS % STAGE_SLOTS == 0 and len(MIX_LOADS) % STAGE_SLOTS == 0

LOADED = 64

V_ORDER = (2, 3, 4, 5, 6, 7, 8, 0, 1)
C_ADA, C_NORM, C_POOL, C_QG, C_KG = 0, N_ADA * KT, N_ADA * KT + 3 * KT, N_ADA * KT + 3 * KT + 4, N_ADA * KT + 3 * KT + 5
C_C = C_KG + 1
N_ROWS = C_C + KT

ADA_W = 512
FF_ADA = 3 * KT
MIX_ADA = 3 * 2 * KT
ADA_PIECES = 4 * FF_ADA + MIX_ADA
FF_GROUPS, MIX_GROUPS = 3, 6
ADA_GROUPS = 4 * FF_GROUPS + MIX_GROUPS
FF_STEPS = list(range(FF_ADA))
MIX_STEPS = ([0, 0, 1, 1, 2, 2, 3, 4] + [6, 6] + list(range(7, 13)) + list(range(14, 22))
             + [23, 23, 24, 24, 25, 25, 26, 26] + list(range(29, 37)) + [39, 40, 41, 42, 42, 43, 43, 44])
MIX_SUMS = {5: 0, 22: 2, 28: 3, 38: 4, 46: 5}
MIX_SUM_MIDDLE = {14: 1}

NEWTON = 12
VEC_STEPS = 2 + 3 * 3
FH = S // 2
HX = KT + 1
U_STEPS = 2 * KT
FIRST = AHEAD
OUT_BANKS = 4
QK = (T_K, 0, 1, 2, 3)
ATT0 = T_P + 6
SOFT = 6 * N_CHUNKS


def soft_a(a):
    return 6 * a + 3


K_ID, K_SWAP, K_HEADS, K_FREQ, K_SIGN, K_CNT = 0, P, 2 * P, 2 * P + 2, 2 * P + 3, 2 * P + 4
K_W = K_CNT + len(POOL_WINDOWS) * PAD

TWO_PI_1 = 6.28125
TWO_PI_2 = float(np.float32(np.round((2 * np.pi - TWO_PI_1) * 2.0**20) / 2.0**20))
TWO_PI_3 = float(np.float32(2 * np.pi - TWO_PI_1 - TWO_PI_2))
ROUND = 12582912.0
SIN_MAX = 3.1415925


def shape_constants():
    k = np.zeros((P, K_W), np.float32)
    row = np.arange(P)
    k[row, K_ID + row] = 1.0
    k[row, K_SWAP + (row // HEAD) * HEAD + (row % HEAD + HEAD // 2) % HEAD] = 1.0
    k[row, K_HEADS + row // HEAD] = 1.0
    inv = (ROPE_THETA ** (-np.arange(0, HEAD, 2, dtype=np.float64) / HEAD)).astype(np.float32)
    k[:, K_FREQ] = inv[row % (HEAD // 2)]
    k[:, K_SIGN] = np.where(row % HEAD < HEAD // 2, -1.0, 1.0)
    for g, w in enumerate(POOL_WINDOWS):
        k[:, K_CNT + g * PAD:K_CNT + (g + 1) * PAD] = 1.0 / np.minimum(np.arange(PAD) + 1, w)
    return k


def trunk(nc, x, c, positions, w_ada, b_ada, norm_g, w_ff1_up, w_ff1_down, w_in, q_norm_g, k_norm_g,
          sinks, w_pool_grp, pool_scale, w_attn_o, w_pool_o, w_out, w_ff2_up, w_ff2_down, consts, out):
    ctx = ExitStack()
    with ctx:
        place = [nc.sbuf_base + (-nc.sbuf_base) % 64]

        def region(nbytes):
            at = place[0]
            place[0] += nbytes + (-nbytes) % 32
            return at

        def at(name, shape, dt, offset):
            return nc.alloc_sbuf_tensor_at(name, shape, dt, offset=offset)

        KB2 = S * 4
        r_stage = region(STAGE_SLOTS * STAGE_W * 4)
        r_hi = region(BANKS * HI_W * 4)
        r_x = region(KT * KB2)
        r_u = region(2 * KT * KB2)
        r_h = region(2 * HALF_FT * KB2)
        r_g = region(KT * KB2)
        r_e = region(4 * KB2)
        r_a = region(3 * (PAD + S) * 4)
        r_misc = region(7 * KB2)

        stage = [at(f"stage{s}", [P, STAGE_W], F32, r_stage + s * STAGE_W * 4) for s in range(STAGE_SLOTS)]
        w_lo = [at(f"w_lo{s}", [P, STAGE_W], F32R, r_stage + s * STAGE_W * 4) for s in range(STAGE_SLOTS)]
        w_hi = [at(f"w_hi{s}", [P, HI_W], F32R, r_hi + s * HI_W * 4) for s in range(BANKS)]
        x_t = at("x_t", [P, KT, S], F32, r_x)
        u_hi = at("u_hi", [P, KT, S], F32R, r_u)
        u_lo = at("u_lo", [P, KT, S], F32R, r_u + KT * KB2)
        x_rows = at("x_rows", [P, JT, D], F32, r_u)
        out_rows = at("out_rows", [P, JT, D], F32, r_u + KT * KB2)
        h_hi = at("h_hi", [P, HALF_FT, S], F32R, r_h)
        h_lo = at("h_lo", [P, HALF_FT, S], F32R, r_h + HALF_FT * KB2)
        LO = HALF_FT - KT
        q_rot = at("q_rot", [P, N_CHUNKS, QPK, CHUNK], F32, r_h + KT * KB2)
        k_rot = at("k_rot", [P, N_KV, S], F32, r_h + (KT + QPK) * KB2)
        first_at = [r_h + s * D * 4 for s in range(HALF_FT)] + [r_u + (KT + 2 * s) * KB2 for s in range(4)] + [r_e]
        ada_first = [at(f"ada_first{s}", [P, D], F32, first_at[s]) for s in range(2 * KT)]
        gate_a = at("gate_a", [P, KT, S], F32, r_g)
        qk_raw = at("qk_raw", [P, 5, S], F32, r_g + 3 * KB2)
        silu = at("silu", [P, 2, S], F32, r_g)
        prod = at("prod", [P, 2, S], F32, r_g + 2 * KB2)
        xn = at("xn", [P, 4, FH], F32, r_g + 4 * KB2)
        u_f = at("u_f", [P, 4, FH], F32, r_g + 6 * KB2)
        rope_a = at("rope_a", [P, S], F32, r_e)
        rope_b = at("rope_b", [P, S], F32, r_e + KB2)
        rstd_b = at("rstd_b", [P, S], F32, r_e + 2 * KB2)
        pool_y = at("pool_y", [P, S], F32, r_e + 3 * KB2)
        v_t = at("v_t", [P, S], F32, r_e + 3 * KB2)
        merge = at("merge", [P, 2, S], F32, r_e)
        gate_p = ([at(f"gate_p{i}", [P, S], F32, r_stage + i * STAGE_W * 4 + KT * 2 * P * 4) for i in range(3)]
                  + [at(f"gate_p{3 + i}", [P, S], F32, r_e + (2 + i) * KB2) for i in range(2)]
                  + [at(f"gate_p{5 + i}", [P, S], F32, r_a + i * KB2) for i in range(3)])
        pool_in = [at(f"pool_in{i}", [P, PAD + S], F32, o) for i, o in enumerate((r_a, r_stage + KT * 2 * P * 4))]
        pool_s = [at(f"pool_s{i}", [P, PAD + S], F32, r_a + (1 + i) * (PAD + S) * 4) for i in range(2)]
        probs = [at(f"probs{i}", [P, 4, P], F32, r_a + i * KB2) for i in range(2)]
        probs_t = at("probs_t", [P, 4 * P], F32, r_a + 2 * KB2)
        r = r_misc
        cos_t = at("cos_t", [P, S], F32, r)
        sin_t = at("sin_t", [P, S], F32, r + KB2)
        squares = at("squares", [P, S], F32, r + 2 * KB2)
        sq_sum = at("sq_sum", [P, S], F32, r + 3 * KB2)
        v_win = at("v_win", [P, N_CHUNKS, P], F32, r + 4 * KB2)
        pool_w = at("pool_w", [P, 4, P], F32, r + 6 * KB2)
        ada_stage = [at(f"ada_stage{i}", [P, ADA_W], F32, region(ADA_W * 4)) for i in range(2)]
        ada_acc = at("ada_acc", [P, ADA_W], F32, region(ADA_W * 4))
        ada_acc0 = at("ada_acc0", [P, D], F32, r + 4 * KB2)
        consts_s = at("consts_s", [P, K_W], F32, region(K_W * 4))
        ones = at("ones", [P, 1], F32, region(32))
        rows = at("rows", [P, DEPTH, P], F32, r_g)
        pos_i = at("pos_i", [P, S], I32, r_g + KB2)
        angle = at("angle", [P, S], F32, r_g + 2 * KB2)
        turns = at("turns", [P, S], F32, r_g + 3 * KB2)
        vec = at("vec", [P, DEPTH, N_ROWS], F32, region(DEPTH * N_ROWS * 4))
        lay = at("lay", [P, N_ROWS], F32, region(N_ROWS * 4))
        sink_all = at("sink_all", [P, DEPTH, 4], F32, region(DEPTH * 16))
        neg_sink = at("neg_sink", [P, 4], F32, region(32))
        c_act = at("c_act", [P, KT], F32, region(KT * 4))
        ada_sum = at("ada_sum", [P, N_ADA * KT], F32, region(N_ADA * KT * 4))
        shift_b = at("shift_b", [P, 3, 2, KT], F32, region(6 * KT * 4))
        gate_v = at("gate_v", [P, KT], F32, region(KT * 4))
        scale = at("scale", [P, 3, KT], F32, region(3 * KT * 4))
        gate = at("gate", [P, 3, KT], F32, region(3 * KT * 4))
        nw_v = at("nw_v", [P, 40], F32, region(160))
        nw_y = at("nw_y", [P, 40], F32, region(160))
        nw_t = at("nw_t", [P, 40], F32, region(160))
        neg_max = at("neg_max", [P, 2, 4], F32, region(32))
        row_max = at("row_max", [P, 4], F32, region(32))
        sink_d = at("sink_d", [P, 2, 4], F32, region(32))
        e_sum = at("e_sum", [P, 2, 4], F32, region(32))
        e_sink = at("e_sink", [P, 2, 4], F32, region(32))
        den = at("den", [P, 4], F32, region(32))
        inv_den = at("inv_den", [P, 4], F32, region(32))
        edge = at("edge", [P, PAD], F32, region(PAD * 4))
        assert place[0] <= nc.sbuf_usable_end, (place[0], nc.sbuf_usable_end)

        ident = consts_s[:, K_ID:K_ID + P]
        swap = consts_s[:, K_SWAP:K_SWAP + P]
        heads = consts_s[:, K_HEADS:K_HEADS + 2]

        bank = [ctx.enter_context(nc.psum_tensor(f"bank{i}", [P, S], F32)) for i in range(BANKS)]
        ps5, ps6, ps7 = [ctx.enter_context(nc.psum_tensor(f"ps{i}", [P, S], F32)) for i in (5, 6, 7)]

        def sem(name):
            return ctx.enter_context(nc.semaphore(name))

        consts_in = sem("consts_in")
        late_in = sem("late_in")
        x_in = sem("x_in")
        ada_first_in = [sem(f"ada_first_in{s}") for s in range(2 * KT)]
        loaded = [sem(f"loaded{s}") for s in range(STAGE_SLOTS)]
        ada_in = [sem(f"ada_in{i}") for i in range(2)]
        pool_w_in = sem("pool_w_in")
        hi_ready = sem("hi_ready")
        lo_ready = sem("lo_ready")
        tile_done = sem("tile_done")
        product_ready = sem("product_ready")
        silu_ready = sem("silu_ready")
        h_hi_ready = sem("h_hi_ready")
        h_lo_ready = sem("h_lo_ready")
        x_updated = sem("x_updated")
        squared = sem("squared")
        squares_added = sem("squares_added")
        norm_summed = sem("norm_summed")
        newton = sem("newton")
        rstd_spread = sem("rstd_spread")
        xn_ready = sem("xn_ready")
        u_f_ready = sem("u_f_ready")
        u_hi_ready = sem("u_hi_ready")
        u_lo_ready = sem("u_lo_ready")
        half_done = sem("half_done")
        gate_step = sem("gate_step")
        vec_step = sem("vec_step")
        ada_used = sem("ada_used")
        ada_reduced = sem("ada_reduced")
        ada_added = sem("ada_added")
        mix_read = sem("mix_read")
        gate_read = sem("gate_read")
        qk_squared = sem("qk_squared")
        qk_summed = sem("qk_summed")
        v_turned = sem("v_turned")
        v_kept = sem("v_kept")
        rstd_copied = sem("rstd_copied")
        qk_spread = sem("qk_spread")
        qk_normed = sem("qk_normed")
        qk_swapped = sem("qk_swapped")
        rope_step = sem("rope_step")
        pads_zeroed = sem("pads_zeroed")
        pool_step = sem("pool_step")
        pool_mixed = sem("pool_mixed")
        pool_grouped = sem("pool_grouped")
        pool_y_step = sem("pool_y_step")
        scored = sem("scored")
        soft_step = sem("soft_step")
        exp_ready = sem("exp_ready")
        probs_zeroed = sem("probs_zeroed")
        probs_turned = sem("probs_turned")
        probs_kept = sem("probs_kept")
        attended = sem("attended")
        attn_step = sem("attn_step")
        merge_step = sem("merge_step")
        turned = sem("turned")
        turned_kept = sem("turned_kept")
        turned_kept_act = sem("turned_kept_act")
        first_reduced = sem("first_reduced")
        setup_step = sem("setup_step")
        ada_first_used = sem("ada_first_used")
        act_step = sem("act_step")
        rows_turned = sem("rows_turned")
        stored = sem("stored")

        def tiles_before(l, i, half=0):
            return l * TILES + (0, 2 * FF_TILES, 2 * FF_TILES + MIX_TILES)[i] + half * FF_TILES

        def loads_before(l, i, half=0):
            per = (0, 2 * FF_LOADS, 2 * FF_LOADS + len(MIX_LOADS))
            return l * (LOADS // STAGE_SLOTS) + per[i] // STAGE_SLOTS + half * (FF_LOADS // STAGE_SLOTS)

        def x_before(l, i, half=0):
            return HX * (1 + l * 5 + (0, 2, 3)[i] + half)

        def adds_before(l, i, half=0):
            return (KT - 2) + l * 5 * (KT - 2) + (0, 2, 3)[i] * (KT - 2) + half * (KT - 2)

        def products_before(l, i, half):
            return l * 4 * HALF_FT + (0, 0, 2)[i] * HALF_FT + half * HALF_FT

        def pieces_before(l, i, half=0):
            return l * ADA_PIECES + (0, 2 * FF_ADA, 2 * FF_ADA + MIX_ADA)[i] + half * FF_ADA

        def groups_before(l, i, half=0):
            return l * ADA_GROUPS + (0, 2 * FF_GROUPS, 2 * FF_GROUPS + MIX_GROUPS)[i] + half * FF_GROUPS

        def sums_before(l, i, half=0):
            return 8 * l + (2, 5, 7)[i] + half

        CALLS = 9

        def newton_before(call):
            return call * NEWTON

        def first_call(l, i, half=0):
            return CALLS * l + (2, 6, 8)[i] + half

        DONE = BANKS + 1

        def ff_load_of(n):
            return n // 2, n % 2

        MIX_LOAD_OF = {t + j: (i, j) for i, (t, k) in enumerate(MIX_LOADS) for j in range(k)}

        def depth(kind, n):
            if kind == "ff":
                return KT if n < 2 * HALF_FT or n >= FF_TILES else HALF_FT
            return QPK if T_Y <= n < T_OUT else KT

        def slot_of(kind, n):
            if kind == "ff" or n >= MIX_TILES:
                if kind == "mix":
                    i, j = ff_load_of(n - MIX_TILES)
                    i += len(MIX_LOADS)
                else:
                    i, j = ff_load_of(n)
            else:
                i, j = MIX_LOAD_OF[n]
            return i % STAGE_SLOTS, i // STAGE_SLOTS + 1, j

        def stage_tile(t, kind, n):
            s, _, j = slot_of(kind, n)
            k = depth(kind, n)
            return t[s][:, 0:k * 2 * P].rearrange("p (k c) -> p k c", c=2 * P)[:, :, j * P:(j + 1) * P]

        def hi_tile(n, k):
            return w_hi[n % BANKS][:, 0:k * P].rearrange("p (k c) -> p k c", c=P)

        N_CONSTS = 16 * 10
        N_LATE = 16 * (2 * DEPTH + 1)

        block = ctx.enter_context(nc.Block())

        @block.sync
        def _(sp):
            def ff_half(l, i, half, up, down):
                up_v = up.rearrange("l (k p) n -> l p k n", p=P)
                down_v = down.rearrange("l (f p) n -> l p f n", p=P)
                sent = 0
                for n in range(FF_LOADS):
                    s = n % STAGE_SLOTS
                    dst = stage[s][:, :].rearrange("p (k c) -> p k c", c=2 * P)
                    sp.wait_ge(tile_done, tiles_before(l, i, half) + 2 * n - 5 + DONE)
                    if n < HALF_FT:
                        for j in range(2):
                            sp.dma_start(dst[:, 0:KT, j * P:(j + 1) * P],
                                         up_v[l, :, :, bass.ds((half * HALF_FT + n) * P + j * D_FF, P)]
                                         ).then_inc(loaded[s], LOADED // 2)
                    else:
                        m = 2 * (n - HALF_FT)
                        sp.dma_start(dst[:, :, :], down_v[l, :, bass.ds(half * HALF_FT, HALF_FT), m * P:(m + 2) * P]
                                     ).then_inc(loaded[s], LOADED)
                    while sent < FF_ADA and FF_STEPS[max(sent - 2, 0)] + 4 <= 2 * n:
                        ada_piece(l, i, half, sent)
                        sent += 1
                assert sent == FF_ADA

            def ada_piece(l, i, half, a):
                g, k = divmod(a, KT)
                src = w_ada.rearrange("l (k p) n -> l k p n", p=P)
                free = pieces_before(l, i, half) + a + 1
                first = V_ORDER[3 * i] * D
                if i < 2:
                    sp.wait_ge(ada_used, free)
                    sp.dma_start(ada_stage[a % 2][:, :], src[l, k, :, bass.ds(first + g * ADA_W + half * 3 * ADA_W, ADA_W)]
                                 ).then_inc(ada_in[a % 2], 16)
                    return

                def next_layer(column):
                    with sp.If(l < DEPTH - 1):
                        sp.wait_ge(ada_used, free)
                        sp.dma_start(ada_stage[a % 2][:, :], src[DEPTH - 1, k, :, column]).then_inc(ada_in[a % 2], 16)
                    with sp.Else():
                        sp.wait_ge(ada_used, free)
                        sp.sem_inc(ada_in[a % 2], 16)

                if g < 2:
                    with sp.If(half < 1):
                        sp.wait_ge(ada_used, free)
                        sp.dma_start(ada_stage[a % 2][:, :], src[l, k, :, first + g * ADA_W:first + (g + 1) * ADA_W]
                                     ).then_inc(ada_in[a % 2], 16)
                    with sp.Else():
                        next_layer(slice((g + 1) * ADA_W, (g + 2) * ADA_W))
                else:
                    next_layer(bass.ds(half * 3 * ADA_W, ADA_W))

            def mix(l):
                in_v = w_in.rearrange("l (k p) n -> l p k n", p=P)
                ao_v = w_attn_o.rearrange("l (g t p) n -> l g p t n", g=N_KV, p=HEAD)
                po_v = w_pool_o.rearrange("l (g p) n -> l p g n", p=P)
                out_v = w_out.rearrange("l (k p) n -> l p k n", p=P)
                sent = 0
                for n, (t, k) in enumerate(MIX_LOADS):
                    s = n % STAGE_SLOTS
                    dst = stage[s][:, 0:KT * 2 * P].rearrange("p (k c) -> p k c", c=2 * P)
                    if n < STAGE_SLOTS:
                        last = 2 * n - 5
                    else:
                        last = sum(MIX_LOADS[n - STAGE_SLOTS]) - 1
                    sp.wait_ge(tile_done, tiles_before(l, 1) + last + DONE)
                    if t < T_K:
                        for j in range(2):
                            for g in range(N_KV):
                                col = Q_OFF + (g * QPK + t + j) * HEAD
                                sp.dma_start(dst[:, :, j * P + g * HEAD:j * P + (g + 1) * HEAD],
                                             in_v[l, :, :, col:col + HEAD]).then_inc(loaded[s], LOADED // 4)
                    elif t < T_Y:
                        col = {T_K: K_OFF}.get(t, P_OFF + (t - T_P) * P)
                        sp.dma_start(dst[:, :, 0:k * P], in_v[l, :, :, col:col + k * P]).then_inc(loaded[s], LOADED)
                    elif t < T_OUT:
                        m = (t - T_Y) // 2
                        for g in range(N_KV):
                            sp.dma_start(dst[g * HEAD:(g + 1) * HEAD, 0:QPK, 0:P],
                                         ao_v[l, g, :, :, m * P:(m + 1) * P]).then_inc(loaded[s], LOADED // 4)
                        sp.dma_start(dst[:, 0:4, P:2 * P], po_v[l, :, :, m * P:(m + 1) * P]
                                     ).then_inc(loaded[s], LOADED // 2)
                    else:
                        sp.dma_start(dst[:, :, :], out_v[l, :, :, (t - T_OUT) * P:(t - T_OUT + 2) * P]
                                     ).then_inc(loaded[s], LOADED)
                    if n == 0:
                        sp.dma_start(pool_w[:, :, :], w_pool_grp.rearrange("l g i o -> l i g o")[l]
                                     ).then_inc(pool_w_in, 16)
                    while sent < MIX_ADA and MIX_STEPS[max(sent - 2, 0)] + 3 <= t:
                        ada_piece(l, 1, 0, sent)
                        sent += 1
                while sent < MIX_ADA:
                    ada_piece(l, 1, 0, sent)
                    sent += 1

            for j in range(JT):
                sp.dma_start(x_rows[:, j, :], x[0, j * P:(j + 1) * P, :]).then_inc(x_in, 16)
            sp.wait_ge(consts_in, N_CONSTS)
            for k in range(KT):
                for v in range(2):
                    sp.dma_start(ada_first[2 * k + v][:, :], w_ada[0, k * P:(k + 1) * P, v * D:(v + 1) * D]
                                 ).then_inc(ada_first_in[2 * k + v], 16)

            with sp.Fori(0, DEPTH) as l:
                with sp.Fori(0, 2) as half:
                    ff_half(l, 0, half, w_ff1_up, w_ff1_down)
                mix(l)
                with sp.Fori(0, 2) as half:
                    ff_half(l, 2, half, w_ff2_up, w_ff2_down)
            for s in range(2):
                sp.wait_ge(tile_done, DEPTH * TILES + 2 * s - 5 + DONE)
                sp.dma_start(stage[s][:, 0:KT * 2 * P].rearrange("p (k c) -> p k c", c=2 * P),
                             w_out.rearrange("l (k p) n -> l p k n", p=P)[0, :, :, 0:2 * P]).then_inc(loaded[s], LOADED)
            for t in range(2 * JT):
                h, j = divmod(t, JT)
                sp.wait_ge((turned_kept, turned_kept_act)[t % 2], t // 2 + 1)
                half = slice(h * D // 2, (h + 1) * D // 2)
                sp.dma_start(out[0, j * P:(j + 1) * P, half], out_rows[:, j, half]).then_inc(stored, 16)
            sp.wait_ge(stored, 16 * 2 * JT)
            for s in range(2):
                sp.wait_ge(loaded[s], LOADED * (DEPTH * LOADS // STAGE_SLOTS + 1))

        @block.gpsimd
        def _(pool):
            def low_part(kind, base, n):
                pool.wait_ge(hi_ready, base + n + 1)
                t = stage_tile(stage, kind, n)
                nc.gpsimd.tensor_tensor(stage_tile(w_lo, kind, n), t, hi_tile(n, depth(kind, n)),
                                        ALU.subtract).then_inc(lo_ready, 1)

            def window_sums(l, g):
                pool.wait_ge(mix_read, l * 26 + T_P + g + 1)
                if g:
                    pool.wait_ge(pool_mixed, (l * 4 + g) * 3)
                src = pool_in[g % 2]
                for i in range(g + 1):
                    step = 1 << i
                    done = l * 10 + g * (g + 1) // 2 + i
                    if i:
                        pool.wait_ge(pool_step, done)
                    nc.gpsimd.tensor_tensor(pool_s[i % 2][:, PAD:], src[:, PAD:], src[:, PAD - step:PAD + S - step],
                                            ALU.add).then_inc(pool_step, 1)
                    src = pool_s[i % 2]

            def u_low(l, i):
                for q in range(U_STEPS):
                    h, k = divmod(q, KT)
                    pool.wait_ge(u_hi_ready, (l * 3 + i) * U_STEPS + q + 1)
                    nc.gpsimd.tensor_tensor(u_lo[:, k, h * FH:(h + 1) * FH], u_f[:, q % 4, :],
                                            u_hi[:, k, h * FH:(h + 1) * FH], ALU.subtract).then_inc(u_lo_ready, 1)

            nc.gpsimd.memset(ones[:, :], 1.0).then_inc(pads_zeroed, 1)
            for n in range(1, AHEAD):
                low_part("ff", 0, n)
            with pool.Fori(0, DEPTH) as l:
                u_low(l, 0)
                with pool.Fori(0, 2) as half:
                    for n in range(FF_TILES):
                        low_part("ff", tiles_before(l, 0, half), n + AHEAD)
                u_low(l, 1)
                for n in range(MIX_TILES):
                    low_part("mix", tiles_before(l, 1), n + AHEAD)
                    if n == 1:
                        for t in (*pool_in, *pool_s):
                            nc.gpsimd.memset(t[:, 0:PAD], 0.0).then_inc(pads_zeroed, 1)
                        pool.wait_ge(pads_zeroed, l * 4 + 5)
                    if T_P - 1 <= n < T_P + 3:
                        window_sums(l, n - T_P + 1)
                u_low(l, 2)
                with pool.Fori(0, 2) as half:
                    for n in range(FF_TILES):
                        low_part("ff", tiles_before(l, 2, half), n + AHEAD)

        @block.scalar
        def _(act):
            def round_weights(kind, tiles, loads, n):
                s, count, _ = slot_of(kind, n)
                act.wait_ge(loaded[s], LOADED * (loads + count))
                act.wait_ge(tile_done, tiles + n - BANKS + DONE)
                nc.scalar.activation(hi_tile(n, depth(kind, n)), stage_tile(stage, kind, n), ACT.Copy
                                     ).then_inc(hi_ready, 1)

            def square(x_count, m, adds):
                parts = [(m, slice(0, S))] if m < KT - 1 else [(m, slice(0, FH)), (m + 1, slice(FH, S))]
                for step, frames in parts:
                    act.wait_ge(x_updated, x_count + step + 1)
                    if 1 < m == step:
                        act.wait_ge(squares_added, adds + m - 1)
                    nc.scalar.activation((squares if m else sq_sum)[:, frames], x_t[:, m, frames], ACT.Square
                                         ).then_inc(squared, 1)

            def round_u(l, i):
                for q in range(U_STEPS):
                    h, k = divmod(q, KT)
                    act.wait_ge(u_f_ready, (l * 3 + i) * U_STEPS + q + 1)
                    nc.scalar.activation(u_hi[:, k, h * FH:(h + 1) * FH], u_f[:, q % 4, :], ACT.Copy
                                         ).then_inc(u_hi_ready, 1)

            def ff_half(l, i, half):
                tiles, loads = tiles_before(l, i, half), loads_before(l, i, half)
                for n in range(FF_TILES):
                    round_weights("ff", tiles, loads, n + AHEAD)
                    if n < 2 * HALF_FT and n % 2 == 0:
                        j = n // 2
                        act.wait_ge(tile_done, tiles + n + DONE)
                        if j >= 2:
                            act.wait_ge(product_ready, products_before(l, i, half) + j - 1)
                        nc.scalar.activation(silu[:, j % 2, :], bank[n % BANKS][:, :], ACT.Silu
                                             ).then_inc(silu_ready, 1)
                    if n >= 2 * HALF_FT:
                        square(x_before(l, i, half), n - 2 * HALF_FT, adds_before(l, i, half))

            def attend(l, a):
                if 1 <= a <= N_CHUNKS:
                    act.wait_ge(probs_turned, l * N_CHUNKS + a)
                    nc.scalar.activation(probs_t[:, :], ps6[:, :], ACT.Copy).then_inc(probs_kept, 1)
                if a < N_CHUNKS:
                    keys = slice(0, CHUNK) if a == 0 else slice(0, 2 * CHUNK)
                    act.wait_ge(soft_step, l * SOFT + soft_a(a))
                    for b in range(4):
                        nc.scalar.activation(probs[a % 2][:, b, keys], ps5[:, b * P:(b + 1) * P][:, keys], ACT.Exp,
                                             scale=HEAD ** -0.5, bias=neg_max[:, a % 2, b:b + 1],
                                             accum_out=e_sum[:, a % 2, b:b + 1]).then_inc(exp_ready, 1)
                    nc.scalar.activation(e_sink[:, a % 2, :], sink_d[:, a % 2, :], ACT.Exp).then_inc(exp_ready, 1)

            def mix(l):
                tiles, loads = tiles_before(l, 1), loads_before(l, 1)
                for n in range(MIX_TILES):
                    if not T_P <= n < T_Y:
                        round_weights("mix", tiles, loads, n + AHEAD)
                    if n == T_P:
                        for h in range(2):
                            act.wait_ge(v_turned, l * 2 + h + 1)
                            nc.scalar.activation(v_win[:, 4 * h:4 * h + 4, :].rearrange("p c d -> p (c d)"),
                                                 (ps6, ps7)[h][:, :], ACT.Copy).then_inc(v_kept, 1)
                    if n < 5:
                        act.wait_ge(mix_read, l * 26 + n + 1)
                        if n:
                            act.wait_ge(qk_summed, l * 5 + n)
                        nc.scalar.activation(squares[:, :], qk_raw[:, n, :], ACT.Square).then_inc(qk_squared, 1)
                    if T_GA <= n < T_Y:
                        g = n - T_GA
                        act.wait_ge(tile_done, tiles + n + DONE)
                        dst = gate_a[:, g, :] if g < KT else gate_p[g - KT][:, :]
                        if 3 <= g < KT:
                            act.wait_ge(rope_step, l * 15 + 15)
                        nc.scalar.activation(dst, bank[n % BANKS][:, :], ACT.Tanh, scale=0.5
                                             ).then_inc(gate_read, 1)
                    if ATT0 <= n < ATT0 + N_CHUNKS + 2:
                        attend(l, n - ATT0)
                    if T_P <= n < T_Y:
                        round_weights("mix", tiles, loads, n + AHEAD)
                    if n >= T_OUT:
                        square(x_before(l, 1), n - T_OUT, adds_before(l, 1))

            act.dma_start(consts_s[:, :], consts).then_inc(consts_in, 16)
            act.dma_start(rows[C_C:C_C + KT, 0, :], c.rearrange("b (r c) -> (b r) c", c=P)).then_inc(consts_in, 16)
            b_rows = b_ada.rearrange("l (r c) -> r l c", c=P)
            cut = (N_ADA - 2) * KT
            act.dma_start(rows[C_ADA:C_ADA + cut, :, :], b_rows[2 * KT:]).then_inc(consts_in, 16)
            act.dma_start(rows[C_ADA + cut:C_NORM, :, :], b_rows[0:2 * KT]).then_inc(consts_in, 16)
            for i in range(DEPTH):
                act.dma_start(rows[C_NORM:C_POOL, i, :], norm_g[i].rearrange("n (r c) -> (n r) c", c=P)
                              ).then_inc(consts_in, 16)
            act.dma_start(rows[C_POOL:C_QG, :, :], pool_scale.rearrange("l (r c) -> r l c", c=P)).then_inc(consts_in, 16)
            for row, src in ((C_QG, q_norm_g), (C_KG, k_norm_g)):
                twice = src.rearrange("l (o c) -> o l c", o=1).unsqueeze(2).to_broadcast([1, DEPTH, 2, HEAD])
                act.dma_start(rows[row:row + 1, :, :].rearrange("p l (g c) -> p l g c", g=2), twice
                              ).then_inc(consts_in, 16)
            act.dma_start(rows[C_C:C_C + KT, 1, :], c.rearrange("b (r c) -> (b r) c", c=P)).then_inc(consts_in, 16)
            act.dma_start(pos_i[:, :], positions[0].partition_broadcast(P)).then_inc(late_in, 16)
            with nc.allow_non_contiguous_dma(reason="eight sinks"):
                for i in range(DEPTH):
                    for t in range(2):
                        act.dma_start(sink_all[t * CHUNK:(t + 1) * CHUNK, i, :],
                                      sinks[i].rearrange("(b t) -> t b", t=2)[t].partition_broadcast(CHUNK)
                                      ).then_inc(late_in, 16)
            act.wait_ge(setup_step, DEPTH)
            nc.scalar.activation(c_act[:, :], vec[:, 0, C_C:C_C + KT], ACT.Silu).then_inc(act_step, 1)
            for m in range(KT):
                square(0, m, 0)
            act.wait_ge(setup_step, DEPTH + 8)
            nc.scalar.activation(sin_t[:, :], angle[:, :], ACT.Sin).then_inc(act_step, 1)
            nc.scalar.activation(cos_t[:, :], angle[:, :], ACT.Sin, scale=0.5).then_inc(act_step, 1)
            for n in range(AHEAD):
                s, count, _ = slot_of("ff", n)
                act.wait_ge(loaded[s], LOADED * count)
                nc.scalar.activation(hi_tile(n, KT), stage_tile(stage, "ff", n), ACT.Copy).then_inc(hi_ready, 1)
            with act.Fori(0, DEPTH) as l:
                round_u(l, 0)
                with act.Fori(0, 2) as half:
                    ff_half(l, 0, half)
                round_u(l, 1)
                mix(l)
                round_u(l, 2)
                with act.Fori(0, 2) as half:
                    ff_half(l, 2, half)
            for t in range(1, 2 * JT, 2):
                h, j = divmod(t, JT)
                act.wait_ge(turned, KT + t + 1)
                nc.scalar.activation(out_rows[:, j, h * D // 2:(h + 1) * D // 2], bank[t % OUT_BANKS][:, :], ACT.Copy
                                     ).then_inc(turned_kept_act, 1)

        @block.vector
        def _(dve):
            def rsqrt_step(count, src, columns, over, step):
                v, y, t = nw_v[:, columns], nw_y[:, columns], nw_t[:, columns]
                if step:
                    dve.wait_ge(newton, count + step)
                if step == 0:
                    ins = nc.vector.tensor_scalar(v, src, 1.0 / over, EPS, ALU.mult, ALU.add)
                elif step == 1:
                    ins = nc.vector.tensor_scalar(y.bitcast(I32), v.bitcast(I32), 1, None, ALU.logical_shift_right)
                elif step == 2:
                    ins = nc.vector.tensor_scalar(y.bitcast(I32), y.bitcast(I32), -1.0, float(0x5F3759DF),
                                                  ALU.mult, ALU.add)
                elif step % 3 == 0:
                    ins = nc.vector.tensor_tensor(t, y, y, ALU.mult)
                elif step % 3 == 1:
                    ins = nc.vector.scalar_tensor_tensor(t, t, -0.5, v, ALU.mult, ALU.mult)
                else:
                    ins = nc.vector.scalar_tensor_tensor(y, t, 1.5, y, ALU.add, ALU.mult)
                ins.then_inc(newton, 1)

            def vectors(l, i):
                count = l * VEC_STEPS + 2 + i * 3
                first = (3 * i - 2) % N_ADA * KT
                dve.wait_ge(ada_added, groups_before(l, i) + 1)
                both = shift_b[:, i, :, :].rearrange("p v k -> p (v k)")
                dve.wait_ge(vec_step, count)
                nc.vector.tensor_tensor(both, ada_sum[:, first:first + 2 * KT], lay[:, C_ADA + first:C_ADA + first + 2 * KT],
                                        ALU.add).then_inc(vec_step, 1)
                dve.wait_ge(vec_step, count + 1)
                nc.vector.scalar_tensor_tensor(scale[:, i, :], shift_b[:, i, 1, :], 1.0,
                                               lay[:, C_NORM + i * KT:C_NORM + (i + 1) * KT], ALU.add, ALU.mult
                                               ).then_inc(vec_step, 1)
                nc.vector.memset(ada_sum[:, first - KT:first + 2 * KT], 0.0).then_inc(vec_step, 1)

            def make_gate(l, i, half):
                at = 3 * i * KT
                count = 10 * l + (0, 4, 6)[i] + 2 * half
                dve.wait_ge(ada_added, groups_before(l, i) + 3)
                nc.vector.tensor_tensor(gate_v[:, :], ada_sum[:, at:at + KT], lay[:, C_ADA + at:C_ADA + at + KT], ALU.add
                                        ).then_inc(gate_step, 1)
                dve.wait_ge(gate_step, count + 1)
                nc.vector.tensor_scalar(gate[:, i, :], gate_v[:, :], 0.5, None, ALU.mult).then_inc(gate_step, 1)
                dve.wait_ge(gate_step, count + 2)

            def stats_step(call, sums, h, step):
                if step == 0:
                    dve.wait_ge(norm_summed, sums)
                rsqrt_step(newton_before(call), ps5[:, 2 * h:2 * h + 2], slice(2 * h, 2 * h + 2), D, step)

            def stats(call, sums, h):
                for step in range(NEWTON):
                    stats_step(call, sums, h, step)

            def normalise(l, i):
                base = (l * 3 + i) * U_STEPS

                def divide(q):
                    h, k = divmod(q, KT)
                    if k == 0:
                        dve.wait_ge(rstd_spread, (l * 3 + i) * 2 + h + 1)
                    if q >= 4:
                        dve.wait_ge(u_f_ready, base + q - 3)
                    frames = slice(h * FH, (h + 1) * FH)
                    nc.vector.tensor_tensor(xn[:, q % 4, :], x_t[:, k, frames], (ps6, ps7)[h][:, frames], ALU.mult
                                            ).then_inc(xn_ready, 1)

                def full(q):
                    h, k = divmod(q, KT)
                    dve.wait_ge(xn_ready, base + q + 1)
                    if q >= 4:
                        dve.wait_ge(u_lo_ready, base + q - 3)
                    nc.vector.tensor_scalar(u_f[:, q % 4, :], xn[:, q % 4, :], scale[:, i, k:k + 1],
                                            shift_b[:, i, 0, k:k + 1], ALU.mult, ALU.add).then_inc(u_f_ready, 1)

                divide(0)
                dve.wait_ge(vec_step, l * VEC_STEPS + 2 + i * 3 + 2)
                full(0)
                for q in range(1, U_STEPS):
                    divide(q)
                    if 2 < q <= 2 + NEWTON // 3:
                        stats_step(CALLS * l + 1 + 3 * i, 8 * l + (1, 4, 6)[i] + 1, 1, 3 * (q - 3))
                    if q > 1:
                        full(q - 1)
                    if 2 < q <= 2 + NEWTON // 3:
                        for step in range(3 * (q - 3) + 1, 3 * (q - 3) + 3):
                            stats_step(CALLS * l + 1 + 3 * i, 8 * l + (1, 4, 6)[i] + 1, 1, step)
                full(U_STEPS - 1)

            def update_x(l, i, half, m, n, tiles):
                x_count, adds = x_before(l, i, half), adds_before(l, i, half)

                def update(product, frames):
                    nc.vector.scalar_tensor_tensor(x_t[:, m, frames], product[:, frames], gate[:, i, m:m + 1],
                                                   x_t[:, m, frames], ALU.mult, ALU.add).then_inc(x_updated, 1)
                if m < KT - 1:
                    dve.wait_ge(tile_done, tiles + n + DONE)
                    update(bank[n % BANKS], slice(0, S))
                    if m >= 2:
                        add_squares(x_count, m - 1, adds)
                    return
                add_squares(x_count, m - 1, adds)
                dve.wait_ge(half_done, 5 * l + (0, 2, 3)[i] + half + 1)
                update(ps6, slice(0, FH))
                stats(first_call(l, i, half), sums_before(l, i, half) + 1, 0)
                dve.wait_ge(tile_done, tiles + n + DONE)
                update(bank[n % BANKS], slice(FH, S))

            def add_squares(x_count, m, adds):
                dve.wait_ge(squared, x_count + m + 1)
                if m >= 2:
                    dve.wait_ge(squares_added, adds + m - 1)
                nc.vector.tensor_tensor(sq_sum[:, :], sq_sum[:, :], squares[:, :], ALU.add).then_inc(squares_added, 1)

            def ada_piece(l, i, half, a):
                count, k = pieces_before(l, i, half), a % KT
                dve.wait_ge(ada_in[a % 2], 16 * (l * (ADA_PIECES // 2) + (0, FF_ADA, FF_ADA + MIX_ADA // 2)[i]
                                                 + half * (FF_ADA // 2) + a // 2 + 1))
                c_k = c_act[:, k:k + 1]
                if k == 0:
                    dve.wait_ge(ada_reduced, groups_before(l, i, half) + a // KT + 1)
                    nc.vector.tensor_scalar(ada_acc[:, :], ada_stage[a % 2][:, :], c_k, None, ALU.mult
                                            ).then_inc(ada_used, 1)
                else:
                    dve.wait_ge(ada_used, count + a + 2)
                    nc.vector.scalar_tensor_tensor(ada_acc[:, :], ada_stage[a % 2][:, :], c_k, ada_acc[:, :],
                                                   ALU.mult, ALU.add).then_inc(ada_used, 1)

            def ada_group(l, i, half, g):
                count = groups_before(l, i, half) + g
                dve.wait_ge(ada_reduced, count + 2)
                s = ada_sum[:, bass.ds(3 * i * KT + 4 * g + half * 12, 4)]
                nc.vector.tensor_tensor(s, s, ps7[:, 0:4], ALU.add).then_inc(ada_added, 1)

            def ff_half(l, i, half):
                tiles = tiles_before(l, i, half)
                count = products_before(l, i, half)
                for n in range(FF_TILES):
                    if n < 2 * HALF_FT and n % 2 == 1:
                        j = n // 2
                        dve.wait_ge(silu_ready, count + j + 1)
                        dve.wait_ge(tile_done, tiles + n + DONE)
                        if j:
                            dve.wait_ge(h_lo_ready, count + j)
                        nc.vector.tensor_tensor(prod[:, j % 2, :], silu[:, j % 2, :], bank[n % BANKS][:, :], ALU.mult
                                                ).then_inc(product_ready, 1)
                        dve.wait_ge(product_ready, count + j + 1)
                        nc.vector.tensor_copy(h_hi[:, j, :], prod[:, j % 2, :]).then_inc(h_hi_ready, 1)
                        dve.wait_ge(h_hi_ready, count + j + 1)
                        nc.vector.tensor_tensor(h_lo[:, j, :], prod[:, j % 2, :], h_hi[:, j, :], ALU.subtract
                                                ).then_inc(h_lo_ready, 1)
                    if n >= 2 * HALF_FT:
                        update_x(l, i, half, n - 2 * HALF_FT, n, tiles)
                    if n and n % 8 == 0 and n // 8 <= FF_GROUPS:
                        ada_group(l, i, half, n // 8 - 1)
                    if n == 18:
                        make_gate(l, i, half)
                    if n < FF_ADA:
                        ada_piece(l, i, half, n)

            def read_tile(tiles, n, dst):
                dve.wait_ge(tile_done, tiles + n + DONE)
                nc.vector.tensor_copy(dst, bank[n % BANKS][:, :]).then_inc(mix_read, 1)

            def widen_rstd(l, i):
                if i:
                    dve.wait_ge(qk_spread, l * 5 + i)
                nc.vector.tensor_copy(rstd_b[:, :].rearrange("p (j c) -> p j c", c=HEAD),
                                      nw_y[:, 8 * QK[i]:8 * QK[i] + 8].unsqueeze(2).to_broadcast([P, 8, HEAD])
                                      ).then_inc(rstd_copied, 1)

            def norm_qk(l, i):
                dve.wait_ge(qk_spread, l * 5 + i + 1)
                g = C_KG if QK[i] == T_K else C_QG
                raw = qk_raw[:, QK[i], :]
                nc.vector.scalar_tensor_tensor(raw, ps6[:, :], lay[:, g:g + 1], raw, ALU.mult, ALU.mult
                                               ).then_inc(qk_normed, 1)

            def rope(l, i):
                count = l * 15 + 3 * i
                if i:
                    dve.wait_ge(rope_step, count)
                dve.wait_ge(qk_swapped, l * 5 + i + 1)
                nc.vector.tensor_tensor(rope_a[:, :], qk_raw[:, QK[i], :], cos_t[:, :], ALU.mult
                                        ).then_inc(rope_step, 1)
                nc.vector.tensor_tensor(rope_b[:, :], ps7[:, :], sin_t[:, :], ALU.mult).then_inc(rope_step, 1)
                dve.wait_ge(rope_step, count + 2)
                if QK[i] == T_K:
                    for g in range(N_KV):
                        r = slice(g * HEAD, (g + 1) * HEAD)
                        ins = nc.vector.tensor_tensor(k_rot[r, g, :], rope_a[r, :], rope_b[r, :], ALU.add)
                    ins.then_inc(rope_step, 1)
                else:
                    v = "p (c q) -> p c q"
                    nc.vector.tensor_tensor(q_rot[:, :, QK[i], :], rope_a[:, :].rearrange(v, q=CHUNK),
                                            rope_b[:, :].rearrange(v, q=CHUNK), ALU.add).then_inc(rope_step, 1)

            def pool_mix(l, g):
                dve.wait_ge(pool_step, l * 10 + (g + 1) * (g + 2) // 2)
                s, own, count = pool_s[g % 2], pool_in[g % 2], (l * 4 + g) * 3
                nc.vector.tensor_tensor(edge[:, :], s[:, PAD:2 * PAD], consts_s[:, K_CNT + g * PAD:K_CNT + (g + 1) * PAD],
                                        ALU.mult).then_inc(pool_mixed, 1)
                nc.vector.scalar_tensor_tensor(own[:, 2 * PAD:], s[:, 2 * PAD:], 1.0 / POOL_WINDOWS[g],
                                               own[:, 2 * PAD:], ALU.mult, ALU.subtract).then_inc(pool_mixed, 1)
                dve.wait_ge(pool_mixed, count + 2)
                nc.vector.tensor_tensor(own[:, PAD:2 * PAD], edge[:, :], own[:, PAD:2 * PAD], ALU.subtract
                                        ).then_inc(pool_mixed, 1)

            def pool_out(l, g):
                dve.wait_ge(pool_grouped, l * 4 + g + 1)
                count = (l * 4 + g) * 3
                nc.vector.tensor_scalar(pool_y[:, :], ps5[:, :], lay[:, C_POOL + g:C_POOL + g + 1], None, ALU.mult
                                        ).then_inc(pool_y_step, 1)
                dve.wait_ge(pool_y_step, count + 1)
                nc.vector.tensor_copy(h_hi[:, 4 + g, :], pool_y[:, :]).then_inc(pool_y_step, 1)
                dve.wait_ge(pool_y_step, count + 2)
                nc.vector.tensor_tensor(h_lo[:, LO + 4 + g, :], pool_y[:, :], h_hi[:, 4 + g, :], ALU.subtract
                                        ).then_inc(pool_y_step, 1)

            def attend(l, a):
                base = l * SOFT
                if a < N_CHUNKS:
                    keys = slice(0, CHUNK) if a == 0 else slice(0, 2 * CHUNK)
                    at_a = base + soft_a(a)
                    dve.wait_ge(scored, l * N_CHUNKS + a + 1)
                    nc.vector.tensor_reduce(row_max[:, :], ps5[:, :].rearrange("p (b k) -> p b k", k=P)[:, :, keys],
                                            AX_X, ALU.max).then_inc(soft_step, 1)
                    dve.wait_ge(soft_step, at_a - 2)
                    nc.vector.scalar_tensor_tensor(neg_max[:, a % 2, :], row_max[:, :], -(HEAD ** -0.5), neg_sink[:, :],
                                                   ALU.mult, ALU.min).then_inc(soft_step, 1)
                    dve.wait_ge(soft_step, at_a - 1)
                    nc.vector.tensor_tensor(sink_d[:, a % 2, :], neg_max[:, a % 2, :], neg_sink[:, :], ALU.subtract
                                            ).then_inc(soft_step, 1)
                if a >= 2:
                    ch = a - 2
                    dve.wait_ge(attended, l * N_CHUNKS + ch + 1)
                    count = (l * N_CHUNKS + ch) * 4
                    for g in range(N_KV):
                        r = slice(g * HEAD, (g + 1) * HEAD)
                        o = ps7[r, g * 256:(g + 1) * 256].rearrange("p (t q) -> p t q", q=CHUNK)
                        dst = h_hi[r, 0:QPK, ch * CHUNK:(ch + 1) * CHUNK]
                        nc.vector.tensor_copy(dst, o).then_inc(attn_step, 1)
                        dve.wait_ge(attn_step, count + 2 * g + 1)
                        nc.vector.tensor_tensor(h_lo[r, LO:LO + QPK, ch * CHUNK:(ch + 1) * CHUNK], o, dst, ALU.subtract
                                                ).then_inc(attn_step, 1)
                if a < N_CHUNKS:
                    dve.wait_ge(exp_ready, (l * N_CHUNKS + a + 1) * 5)
                    nc.vector.tensor_tensor(den[:, :], e_sum[:, a % 2, :], e_sink[:, a % 2, :], ALU.add
                                            ).then_inc(soft_step, 1)
                    dve.wait_ge(soft_step, at_a + 1)
                    nc.vector.reciprocal(inv_den[:, :], den[:, :]).then_inc(soft_step, 1)
                    dve.wait_ge(soft_step, at_a + 2)
                    p = probs[a % 2][:, :, keys]
                    w = CHUNK if a == 0 else 2 * CHUNK
                    nc.vector.tensor_tensor(p, p, inv_den[:, :].unsqueeze(2).to_broadcast([P, 4, w]), ALU.mult
                                            ).then_inc(soft_step, 1)

            def merged(l, n, tiles):
                m, which = divmod(n - T_Y, 2)
                count = (l * KT + m) * 4
                dve.wait_ge(tile_done, tiles + n + DONE)
                if which == 0:
                    if m == 0:
                        dve.wait_ge(gate_read, (l + 1) * 2 * KT)
                    else:
                        dve.wait_ge(merge_step, count)
                    nc.vector.scalar_tensor_tensor(merge[:, 0, :], gate_a[:, m, :], 1.0, bank[n % BANKS][:, :],
                                                   ALU.add, ALU.mult).then_inc(mix_read, 1)
                    return
                nc.vector.scalar_tensor_tensor(merge[:, 1, :], gate_p[m][:, :], 1.0, bank[n % BANKS][:, :],
                                               ALU.add, ALU.mult).then_inc(mix_read, 1)
                dve.wait_ge(mix_read, l * 26 + 10 + (n - T_Y) + 1)
                nc.vector.tensor_tensor(merge[:, 0, :], merge[:, 0, :], merge[:, 1, :], ALU.add).then_inc(merge_step, 2)
                dve.wait_ge(merge_step, count + 2)
                nc.vector.tensor_copy(u_hi[:, m, :], merge[:, 0, :]).then_inc(merge_step, 1)
                dve.wait_ge(merge_step, count + 3)
                nc.vector.tensor_tensor(u_lo[:, m, :], merge[:, 0, :], u_hi[:, m, :], ALU.subtract
                                        ).then_inc(merge_step, 1)

            def mix(l):
                tiles = tiles_before(l, 1)
                for n in range(MIX_TILES):
                    if T_P + 2 <= n <= T_P + 5:
                        pool_mix(l, n - T_P - 2)
                    if T_P + 1 <= n <= T_P + 4:
                        rope(l, n - T_P - 1)
                        norm_qk(l, n - T_P)
                        if n - T_P + 1 < 5:
                            widen_rstd(l, n - T_P + 1)
                    if n in MIX_SUM_MIDDLE:
                        ada_group(l, 1, 0, MIX_SUM_MIDDLE[n])
                    if n == 0:
                        nc.vector.memset(k_rot[HEAD:, 0, :], 0.0)
                        nc.vector.memset(k_rot[0:HEAD, 1, :], 0.0)
                    if n == T_Y:
                        make_gate(l, 1, 0)
                    if n < 5:
                        read_tile(tiles, n, qk_raw[:, n, :])
                    if n == T_V:
                        read_tile(tiles, n, v_t[:, :])
                        ada_group(l, 1, 0, MIX_SUMS[n])
                        dve.wait_ge(qk_summed, (l + 1) * 5)
                        for step in range(NEWTON):
                            rsqrt_step(newton_before(CALLS * l + 5), ps5[:, 0:40], slice(0, 40), HEAD, step)
                        dve.wait_ge(newton, newton_before(CALLS * l + 6))
                        widen_rstd(l, 0)
                    if T_P <= n < T_P + 4:
                        if n == T_P:
                            dve.wait_ge(pads_zeroed, l * 4 + 5)
                        if n >= T_P + 2:
                            dve.wait_ge(pool_grouped, l * 4 + n - T_P - 1)
                        read_tile(tiles, n, pool_in[n % 2][:, PAD:])
                    if n == T_P:
                        norm_qk(l, 0)
                        widen_rstd(l, 1)
                    if n == T_P + 4:
                        rope(l, 4)
                    if T_P + 2 <= n <= T_P + 5:
                        pool_out(l, n - T_P - 2)
                    if n == ATT0:
                        dve.wait_ge(pool_grouped, (l + 1) * 4)
                        nc.vector.memset(probs[0][:, :, CHUNK:], 0.0).then_inc(probs_zeroed, 1)
                    if ATT0 <= n < ATT0 + N_CHUNKS + 2:
                        attend(l, n - ATT0)
                    if T_Y <= n < T_OUT:
                        merged(l, n, tiles)
                    if n >= T_OUT:
                        update_x(l, 1, 0, n - T_OUT, n, tiles)
                    if n in MIX_SUMS and n != T_V:
                        ada_group(l, 1, 0, MIX_SUMS[n])
                    for a, step in enumerate(MIX_STEPS):
                        if step == n:
                            ada_piece(l, 1, 0, a)

            def angles():
                dve.wait_ge(late_in, N_LATE)
                nc.vector.tensor_copy(angle[:, :], pos_i[:, :]).then_inc(setup_step, 1)
                dve.wait_ge(setup_step, DEPTH + 1)
                nc.vector.tensor_scalar(angle[:, :], angle[:, :], consts_s[:, K_FREQ:K_FREQ + 1], None, ALU.mult
                                        ).then_inc(setup_step, 1)
                dve.wait_ge(setup_step, DEPTH + 2)
                nc.vector.tensor_scalar(turns[:, :], angle[:, :], float(1.0 / (2 * np.pi)), ROUND, ALU.mult, ALU.add
                                        ).then_inc(setup_step, 1)
                dve.wait_ge(setup_step, DEPTH + 3)
                nc.vector.tensor_scalar(turns[:, :], turns[:, :], ROUND, None, ALU.subtract).then_inc(setup_step, 1)
                for i, part in enumerate((TWO_PI_1, TWO_PI_2, TWO_PI_3)):
                    dve.wait_ge(setup_step, DEPTH + 4 + i)
                    nc.vector.scalar_tensor_tensor(angle[:, :], turns[:, :], -part, angle[:, :], ALU.mult, ALU.add
                                                   ).then_inc(setup_step, 1)
                dve.wait_ge(setup_step, DEPTH + 7)
                nc.vector.tensor_scalar(angle[:, :], angle[:, :], SIN_MAX, -SIN_MAX, ALU.min, ALU.max
                                        ).then_inc(setup_step, 1)

            dve.sem_inc(ada_used, 2)
            for l in range(DEPTH):
                dve.wait_ge(rows_turned, l + 1)
                nc.vector.tensor_copy(vec[:, l, :], (ps5, ps6)[l][:, 0:N_ROWS]).then_inc(setup_step, 1)
            for m in range(KT):
                dve.wait_ge(turned, m + 1)
                if m < KT - 1:
                    nc.vector.tensor_copy(x_t[:, m, :], bank[m % 4][:, :]).then_inc(x_updated, 1)
                else:
                    for h in range(2):
                        frames = slice(h * FH, (h + 1) * FH)
                        nc.vector.tensor_copy(x_t[:, m, frames], bank[m % 4][:, frames]).then_inc(x_updated, 1)
                if m >= 2:
                    add_squares(0, m - 1, 0)
            dve.wait_ge(act_step, 1)
            for k in range(KT):
                dve.wait_ge(ada_first_in[2 * k + 1], 16)
                piece = ada_first[2 * k + 1]
                if k == 0:
                    nc.vector.tensor_scalar(ada_acc0[:, :], piece[:, :], c_act[:, k:k + 1], None, ALU.mult
                                            ).then_inc(ada_first_used, 1)
                else:
                    dve.wait_ge(ada_first_used, k)
                    nc.vector.scalar_tensor_tensor(ada_acc0[:, :], piece[:, :], c_act[:, k:k + 1], ada_acc0[:, :],
                                                   ALU.mult, ALU.add).then_inc(ada_first_used, 1)
                if k == 3:
                    angles()
                if k == 5:
                    stats(0, 1, 0)
            nc.vector.memset(ada_sum[:, :], 0.0).then_inc(setup_step, 1)
            dve.wait_ge(setup_step, DEPTH + 9)
            dve.wait_ge(act_step, 3)
            nc.vector.tensor_scalar(sin_t[:, :], sin_t[:, :], consts_s[:, K_SIGN:K_SIGN + 1], None, ALU.mult
                                    ).then_inc(setup_step, 1)
            nc.vector.tensor_tensor(cos_t[:, :], cos_t[:, :], cos_t[:, :], ALU.mult).then_inc(setup_step, 1)
            dve.wait_ge(setup_step, DEPTH + 11)
            nc.vector.tensor_scalar(cos_t[:, :], cos_t[:, :], -2.0, 1.0, ALU.mult, ALU.add).then_inc(setup_step, 1)
            dve.wait_ge(hi_ready, 1)
            nc.vector.tensor_tensor(stage_tile(w_lo, "ff", 0), stage_tile(stage, "ff", 0), hi_tile(0, KT), ALU.subtract
                                    ).then_inc(lo_ready, 1)
            dve.wait_ge(first_reduced, 1)
            nc.vector.tensor_copy(ada_sum[:, (N_ADA - 2) * KT:], ps7[:, 0:2 * KT]).then_inc(ada_added, 1)

            with dve.Fori(0, DEPTH) as l:
                nc.vector.tensor_copy(lay[:, :], vec[:, l, :]).then_inc(vec_step, 1)
                nc.vector.tensor_scalar(neg_sink[:, :], sink_all[:, l, :], -1.0, None, ALU.mult).then_inc(vec_step, 1)
                vectors(l, 0)
                normalise(l, 0)
                with dve.Fori(0, 2) as half:
                    ff_half(l, 0, half)
                vectors(l, 1)
                normalise(l, 1)
                mix(l)
                vectors(l, 2)
                normalise(l, 2)
                with dve.Fori(0, 2) as half:
                    ff_half(l, 2, half)
            for t in range(0, 2 * JT, 2):
                h, j = divmod(t, JT)
                dve.wait_ge(turned, KT + t + 1)
                nc.vector.tensor_copy(out_rows[:, j, h * D // 2:(h + 1) * D // 2], bank[t % OUT_BANKS][:, :]
                                      ).then_inc(turned_kept, 1)

        @block.tensor
        def _(pe):
            mm = nc.tensor.matmul

            def tile(kind, base, n, rhs_hi, rhs_lo, before=None, middle=None):
                k_n = depth(kind, n)
                hi, lo = hi_tile(n, k_n), stage_tile(w_lo, kind, n)
                pe.wait_ge(hi_ready, base + n + 1)
                pe.wait_ge(lo_ready, base + n + 1)
                for k in range(k_n):
                    if before:
                        before(k)
                    mm(bank[n % BANKS][:, :], hi[:, k, :], rhs_hi(k), start=(k == 0), stop=False)
                    mm(bank[n % BANKS][:, :], hi[:, k, :], rhs_lo(k), start=False, stop=False)
                    last = mm(bank[n % BANKS][:, :], lo[:, k, :], rhs_hi(k), start=False, stop=(k == k_n - 1))
                    if middle and k == k_n // 2 - 1:
                        middle()
                last.then_inc(tile_done, 1)

            def u_parts():
                return lambda k: u_hi[:, k, :], lambda k: u_lo[:, k, :]

            def last_tile(kind, base, n, rhs_hi, rhs_lo, stats_of):
                k_n = depth(kind, n)
                hi, lo = hi_tile(n, k_n), stage_tile(w_lo, kind, n)
                pe.wait_ge(hi_ready, base + n + 1)
                pe.wait_ge(lo_ready, base + n + 1)
                for h in range(2):
                    frames = slice(h * FH, (h + 1) * FH)
                    dst = (ps6, bank[n % BANKS])[h][:, frames]
                    for k in range(k_n):
                        mm(dst, hi[:, k, :], rhs_hi(k)[:, frames], start=(k == 0), stop=False)
                        mm(dst, hi[:, k, :], rhs_lo(k)[:, frames], start=False, stop=False)
                        last = mm(dst, lo[:, k, :], rhs_hi(k)[:, frames], start=False, stop=(k == k_n - 1))
                        if h and k == 2:
                            norm_sum(*stats_of, 0)
                    last.then_inc((half_done, tile_done)[h], 1)

            def norm_sum(x_count, adds, h):
                pe.wait_ge(squares_added, adds)
                for j in (2 * h, 2 * h + 1):
                    mm(ps5[:, j:j + 1], sq_sum[:, j * P:(j + 1) * P], ones[:, :], start=(j == 2 * h), stop=False,
                       skip_group_check=True)
                pe.wait_ge(squared, x_count - 1 + h)
                for j in (2 * h, 2 * h + 1):
                    last = mm(ps5[:, j:j + 1], squares[:, j * P:(j + 1) * P], ones[:, :], start=False, stop=True,
                              skip_group_check=True)
                last.then_inc(norm_summed, 1)

            def norm_spread(l, i, h):
                pe.wait_ge(newton, newton_before(CALLS * l + 3 * i + 1 + h))
                if h:
                    pe.wait_ge(ada_added, groups_before(l, i) + 1)
                for j in (2 * h, 2 * h + 1):
                    last = mm((ps6, ps7)[h][:, j * P:(j + 1) * P], nw_y[:, j:j + 1].to_broadcast([P, P]), ident,
                              start=True, stop=True)
                last.then_inc(rstd_spread, 1)

            def first_tiles(l, i, kind, base, half_after):
                pe.wait_ge(x_updated, x_before(l, i) - 3)
                pe.wait_ge(hi_ready, base + FIRST)
                pe.wait_ge(lo_ready, base + FIRST)
                for h in range(2):
                    frames = slice(h * FH, (h + 1) * FH)
                    for k in range(KT):
                        step = (l * 3 + i) * U_STEPS + h * KT + k + 1
                        pe.wait_ge(u_hi_ready, step)
                        for n in range(FIRST):
                            hi, lo = hi_tile(n, KT), stage_tile(w_lo, kind, n)
                            mm(bank[n][:, frames], hi[:, k, :], u_hi[:, k, frames], start=(k == 0), stop=False)
                            mm(bank[n][:, frames], lo[:, k, :], u_hi[:, k, frames], start=False, stop=False)
                        pe.wait_ge(u_lo_ready, step)
                        for n in range(FIRST):
                            last = mm(bank[n][:, frames], hi_tile(n, KT)[:, k, :], u_lo[:, k, frames], start=False,
                                      stop=(k == KT - 1))
                            if h and k == KT - 1:
                                last.then_inc(tile_done, 1)
                        if h == 0 and k == half_after:
                            norm_spread(l, i, 1)

            def norm(l, i, kind):
                norm_spread(l, i, 0)
                norm_sum(x_before(l, i), adds_before(l, i), 1)
                first_tiles(l, i, kind, tiles_before(l, i), 3)

            def ada_reduce(l, i, half, g):
                pe.wait_ge(ada_used, pieces_before(l, i, half) + (g + 1) * KT + 2)
                pe.wait_ge(ada_added, groups_before(l, i, half) + g + 1)
                for m in range(4):
                    last = mm(ps7[:, m:m + 1], ada_acc[:, m * P:(m + 1) * P], ones[:, :], start=True, stop=True)
                last.then_inc(ada_reduced, 1)

            def ff_half(l, i, half):
                base = tiles_before(l, i, half)
                count = products_before(l, i, half)
                x_count = x_before(l, i, half)
                def one(n):
                    if n < BANKS:
                        pe.wait_ge(x_updated, x_count + n - BANKS + n // (BANKS - 1))
                    elif n - BANKS < 2 * HALF_FT:
                        pe.wait_ge(product_ready, count + (n - BANKS) // 2 + 1)
                    else:
                        pe.wait_ge(x_updated, x_count + n - BANKS - 2 * HALF_FT + 1)
                    if n < 2 * HALF_FT:
                        tile("ff", base, n, *u_parts())
                    elif n < FF_TILES - 1:
                        tile("ff", base, n, lambda k: h_hi[:, k, :], lambda k: h_lo[:, k, :],
                             before=(lambda k: pe.wait_ge(h_lo_ready, count + k + 1)) if n == 2 * HALF_FT else None)
                    else:
                        last_tile("ff", base, n, lambda k: h_hi[:, k, :], lambda k: h_lo[:, k, :],
                                  (x_count + HX, adds_before(l, i, half) + KT - 2))
                    if n and n % 8 == 0 and n // 8 <= FF_GROUPS:
                        ada_reduce(l, i, half, n // 8 - 1)

                with pe.If(half > 0):
                    for n in range(FIRST):
                        one(n)
                for n in range(FIRST, FF_TILES):
                    one(n)

            def qk_sum(l, t):
                pe.wait_ge(qk_squared, l * 5 + t + 1)
                for j in range(JT):
                    last = mm(ps5[:, 8 * t + 2 * j:8 * t + 2 * j + 2], squares[:, j * P:(j + 1) * P], heads,
                              start=(t == 0 and j == 0), stop=True, skip_group_check=True)
                last.then_inc(qk_summed, 1)

            def turn_v(l):
                pe.wait_ge(mix_read, l * 26 + T_V + 1)
                pe.wait_ge(ada_added, groups_before(l, 1) + 2)
                for h in range(2):
                    for c in range(4 * h, 4 * h + 4):
                        first = max(c - 1, 0) * CHUNK
                        last = nc.tensor.transpose((ps6, ps7)[h][:, (c % 4) * P:(c % 4 + 1) * P],
                                                   v_t[:, first:first + P], ident)
                    last.then_inc(v_turned, 1)

            def spread_qk(l, i):
                pe.wait_ge(rstd_copied, l * 5 + i + 1)
                if i == 0:
                    pe.wait_ge(v_kept, l * 2 + 2)
                else:
                    pe.wait_ge(qk_normed, l * 5 + i)
                for j in range(JT):
                    last = mm(ps6[:, j * P:(j + 1) * P], rstd_b[:, j * P:(j + 1) * P], ident, start=True, stop=True)
                last.then_inc(qk_spread, 1)

            def swap_qk(l, i):
                pe.wait_ge(qk_normed, l * 5 + i + 1)
                if i:
                    pe.wait_ge(rope_step, l * 15 + 3 * i - 1)
                mm(ps7[:, :], swap, qk_raw[:, QK[i], :], start=True, stop=True).then_inc(qk_swapped, 1)

            def group_pool(l, g):
                pe.wait_ge(pool_mixed, (l * 4 + g + 1) * 3)
                if g == 0:
                    pe.wait_ge(pool_w_in, 16 * (l + 1))
                else:
                    pe.wait_ge(pool_y_step, (l * 4 + g) * 3)
                mm(ps5[:, :], pool_w[:, g, :], pool_in[g % 2][:, PAD:], start=True, stop=True).then_inc(pool_grouped, 1)

            def attend(l, a):
                if a >= 2:
                    ch = a - 2
                    pe.wait_ge(probs_kept, l * N_CHUNKS + ch + 1)
                    if ch:
                        pe.wait_ge(attn_step, (l * N_CHUNKS + ch) * 4)
                    if ch == 0:
                        pe.wait_ge(ada_added, groups_before(l, 1) + 3)
                    mm(ps7[:, :], v_win[:, ch, :], probs_t[:, :], start=True, stop=True).then_inc(attended, 1)
                if 1 <= a <= N_CHUNKS:
                    ch = a - 1
                    pe.wait_ge(soft_step, l * SOFT + soft_a(ch) + 3)
                    if ch == 0:
                        pe.wait_ge(probs_zeroed, l + 1)
                    for b in range(4):
                        last = nc.tensor.transpose(ps6[:, b * P:(b + 1) * P], probs[ch % 2][:, b, :], ident)
                    last.then_inc(probs_turned, 1)
                if a < N_CHUNKS:
                    if a == 0:
                        pe.wait_ge(rope_step, (l + 1) * 15)
                        pe.wait_ge(pool_y_step, (l + 1) * 12)
                    else:
                        pe.wait_ge(exp_ready, (l * N_CHUNKS + a) * 5)
                    first, keys = (0, CHUNK) if a == 0 else ((a - 1) * CHUNK, 2 * CHUNK)
                    for b in range(4):
                        g, pair = divmod(b, 2)
                        last = mm(ps5[:, b * P:b * P + keys], q_rot[:, a, 2 * pair:2 * pair + 2, :],
                                  k_rot[:, g, first:first + keys], start=True, stop=True)
                    last.then_inc(scored, 1)

            def mix(l):
                base, x_count = tiles_before(l, 1), x_before(l, 1)
                for n in range(FIRST, MIX_TILES):
                    o = n - BANKS
                    if o < 0:
                        pe.wait_ge(x_updated, x_count + o + 1)
                    elif o < T_GA:
                        pe.wait_ge(mix_read, l * 26 + o + 1)
                    elif o < T_Y:
                        pe.wait_ge(gate_read, l * 2 * KT + o - T_GA + 1)
                    elif o < T_OUT:
                        pe.wait_ge(mix_read, l * 26 + 10 + o - T_Y + 1)
                    else:
                        pe.wait_ge(x_updated, x_count + o - T_OUT + 1)

                    def middle(n=n):
                        if n == 4:
                            qk_sum(l, 1)
                        if n == 5:
                            qk_sum(l, 3)
                        if n == T_P:
                            turn_v(l)
                        if T_P + 1 <= n <= T_P + 4:
                            swap_qk(l, n - T_P - 1)
                            spread_qk(l, n - T_P)
                        if n in MIX_SUM_MIDDLE:
                            pe.wait_ge(rope_step, (l + 1) * 15)
                            ada_reduce(l, 1, 0, MIX_SUM_MIDDLE[n])

                    before = None
                    if T_Y <= n < T_OUT:
                        part = 4 * ((n - T_Y) % 2)
                        if n == T_Y:
                            pe.wait_ge(attn_step, (l + 1) * N_CHUNKS * 4)
                        rhs = (lambda k, o=part: h_hi[:, o + k, :], lambda k, o=part: h_lo[:, LO + o + k, :])
                    else:
                        rhs = u_parts()
                    if n == T_OUT:
                        before = lambda k: pe.wait_ge(merge_step, (l * KT + k + 1) * 4)
                    if n < MIX_TILES - 1:
                        tile("mix", base, n, *rhs, before=before, middle=middle)
                    else:
                        last_tile("mix", base, n, *rhs, (x_count + HX, adds_before(l, 1) + KT - 2))
                    if n == T_V:
                        ada_reduce(l, 1, 0, MIX_SUMS[n])
                    if 3 <= n <= 5:
                        qk_sum(l, 2 * (n - 3))
                    if n == T_P:
                        spread_qk(l, 0)
                    if T_P + 2 <= n <= T_P + 5:
                        group_pool(l, n - T_P - 2)
                    if n == T_P + 4:
                        swap_qk(l, 4)
                    if ATT0 <= n < ATT0 + N_CHUNKS + 2:
                        attend(l, n - ATT0)
                    if n in MIX_SUMS and n != T_V:
                        if MIX_SUMS[n] == 2:
                            pe.wait_ge(attn_step, (l + 1) * N_CHUNKS * 4)
                        ada_reduce(l, 1, 0, MIX_SUMS[n])

            pe.sem_inc(tile_done, BANKS)
            pe.sem_inc(ada_reduced, 1)
            pe.wait_ge(consts_in, N_CONSTS)
            pe.wait_ge(pads_zeroed, 1)
            for l in range(DEPTH):
                nc.tensor.transpose((ps5, ps6)[l][:, 0:N_ROWS], rows[0:N_ROWS, l, :], ident[0:N_ROWS, 0:N_ROWS]
                                    ).then_inc(rows_turned, 1)
            pe.wait_ge(x_in, 16 * JT)
            for m in range(KT):
                if m >= 4:
                    pe.wait_ge(x_updated, m - 3)
                for j in range(JT):
                    last = nc.tensor.transpose(bank[m % 4][:, j * P:(j + 1) * P], x_rows[:, j, m * P:(m + 1) * P], ident)
                last.then_inc(turned, 1)
            pe.wait_ge(act_step, 1)
            for k in range(KT):
                pe.wait_ge(ada_first_in[2 * k], 16)
                for m in range(KT):
                    mm(ps7[:, m:m + 1], ada_first[2 * k][:, m * P:(m + 1) * P], c_act[:, k:k + 1],
                       start=(k == 0 and m == 0), stop=(k == KT - 1), skip_group_check=True)
                if k == 3:
                    norm_sum(HX, KT - 2, 0)
            pe.wait_ge(ada_first_used, KT)
            for m in range(KT):
                last = mm(ps7[:, KT + m:KT + m + 1], ada_acc0[:, m * P:(m + 1) * P], ones[:, :], start=True, stop=True)
            last.then_inc(first_reduced, 1)

            with pe.Fori(0, DEPTH) as l:
                norm(l, 0, "ff")
                with pe.Fori(0, 2) as half:
                    ff_half(l, 0, half)
                norm(l, 1, "mix")
                mix(l)
                norm(l, 2, "ff")
                with pe.Fori(0, 2) as half:
                    ff_half(l, 2, half)
            for t in range(2 * JT):
                h, j = divmod(t, JT)
                if t == 0:
                    pe.wait_ge(x_updated, x_before(DEPTH, 0) - 1)
                if t == JT:
                    pe.wait_ge(x_updated, x_before(DEPTH, 0))
                if t >= OUT_BANKS:
                    pe.wait_ge((turned_kept, turned_kept_act)[t % 2], (t - OUT_BANKS) // 2 + 1)
                for m in range(4):
                    last = nc.tensor.transpose(bank[t % OUT_BANKS][:, m * P:(m + 1) * P],
                                               x_t[:, 4 * h + m, j * P:(j + 1) * P], ident)
                last.then_inc(turned, 1)


INPUTS = ["x", "c", "positions", "w_ada", "b_ada", "norm_g", "w_ff1_up", "w_ff1_down", "w_in", "q_norm_g",
          "k_norm_g", "sinks", "w_pool_grp", "pool_scale", "w_attn_o", "w_pool_o", "w_out", "w_ff2_up", "w_ff2_down"]


def kernel(**inputs):
    import concourse.bacc as bacc
    from concourse.bass_utils import run_bass_kernel_spmd

    nc = bacc.Bacc("TRN2", target_bir_lowering=False, num_devices=1)
    arrays = {f"in_{name}": np.ascontiguousarray(inputs[name]) for name in INPUTS}
    arrays["in_consts"] = shape_constants()
    args = [nc.dram_tensor(name, a.shape, mybir.dt.from_np(a.dtype), kind="ExternalInput").ap()
            for name, a in arrays.items()]
    out = nc.dram_tensor("out", (1, S, D), F32, kind="ExternalOutput").ap()
    trunk(nc, *args, out)
    result = run_bass_kernel_spmd(nc, [arrays], core_ids=[0])
    return result.results[0]["out"]
```
